# Optimizing a Trainium2 kernel written in Bass

```python
import math
import jax, jax.numpy as jnp
from jax import lax
import numpy as np

D_MODEL = 2048
BATCH = 1
SEQ = 256
DEPTH = 1

MIX_WIDTH = D_MODEL
GROUP_DIM = 128
CONV_WIDTH = MIX_WIDTH // 2
GM_WIDTH = MIX_WIDTH - CONV_WIDTH
CONV_GROUPS = CONV_WIDTH // GROUP_DIM
GM_HEADS = GM_WIDTH // GROUP_DIM
CONV_K = 3
CHUNK = 128
D_FF = 256 * math.ceil(8 * D_MODEL / 3 / 256)
N_MEM = 256
XA_HEADS = 4
XA_HEAD_DIM = D_MODEL // XA_HEADS
IN_COLS = 3 * CONV_WIDTH + 2 * GM_WIDTH
EPS = 1e-6

kernel_name = "hybrid_conv_gmlp_macaron_xattn"

def _rmsnorm(x, g):
    x32 = x.astype(jnp.float32)
    y = x32 * lax.rsqrt(jnp.mean(x32 * x32, axis=-1, keepdims=True) + EPS)
    return (y * g.astype(jnp.float32)).astype(x.dtype)

def _swiglu(x, w_in, w_out):
    gate, up = jnp.split(x @ w_in, 2, axis=-1)
    return (jax.nn.silu(gate) * up) @ w_out

def _causal_dwconv(z, conv_w, conv_b):
    s = z.shape[1]
    zp = jnp.pad(z, ((0, 0), (CONV_K - 1, 0), (0, 0)))
    y = conv_b + conv_w[CONV_K - 1] * z
    for k in range(CONV_K - 1):
        y = y + conv_w[k] * zp[:, k:k + s]
    return y

def _spatial_gating(u, v, g_v, w_s, b_s):
    b, s, _ = v.shape
    vh = v.reshape(b, s // CHUNK, CHUNK, GM_HEADS, GROUP_DIM)
    vh = _rmsnorm(vh, g_v.reshape(GM_HEADS, GROUP_DIM))
    mask = jnp.tril(jnp.ones((CHUNK, CHUNK), dtype=bool))
    w = jnp.where(mask[None], w_s, jnp.zeros_like(w_s)).astype(vh.dtype)
    sg = jnp.einsum('hts,bnshc->bnthc', w, vh) + b_s.T[None, None, :, :, None].astype(vh.dtype)
    return u * sg.reshape(b, s, GM_WIDTH)

def _cross_attention(n, mem_n, w_q, w_k, w_v, w_o):
    b, s, _ = n.shape
    m = mem_n.shape[1]
    q = (n @ w_q).reshape(b, s, XA_HEADS, XA_HEAD_DIM)
    k = (mem_n @ w_k).reshape(b, m, XA_HEADS, XA_HEAD_DIM)
    v = (mem_n @ w_v).reshape(b, m, XA_HEADS, XA_HEAD_DIM)
    scores = jnp.einsum('bshd,bmhd->bhsm', q, k).astype(jnp.float32) * (XA_HEAD_DIM ** -0.5)
    p = jax.nn.softmax(scores, axis=-1).astype(q.dtype)
    o = jnp.einsum('bhsm,bmhd->bshd', p, v).reshape(b, s, XA_HEADS * XA_HEAD_DIM)
    return o @ w_o

def setup_inputs(seed: int = 0) -> dict:
    key = jax.random.key(seed)
    ks = jax.random.split(key, 32)
    f32 = jnp.float32

    def w(k, shape, fan_in):
        return jax.random.normal(k, shape, f32) * (fan_in ** -0.5)

    def gain(k, shape):
        return 1.0 + 0.1 * jax.random.normal(k, shape, f32)

    L = DEPTH
    return {
        "x": jax.random.normal(ks[0], (BATCH, SEQ, D_MODEL), f32),
        "mem": jax.random.normal(ks[1], (BATCH, N_MEM, D_MODEL), f32),
        "g_ffn1": gain(ks[2], (L, D_MODEL)),
        "w_ffn1_in": w(ks[3], (L, D_MODEL, 2 * D_FF), D_MODEL),
        "w_ffn1_out": w(ks[4], (L, D_FF, D_MODEL), D_FF),
        "g_mix": gain(ks[5], (L, D_MODEL)),
        "w_mix_in": w(ks[6], (L, D_MODEL, IN_COLS), D_MODEL),
        "conv_w": w(ks[7], (L, CONV_K, CONV_WIDTH), CONV_K),
        "conv_b": 0.01 * jax.random.normal(ks[8], (L, CONV_WIDTH), f32),
        "g_gm_v": gain(ks[9], (L, GM_WIDTH)),
        "w_spatial": w(ks[10], (L, GM_HEADS, CHUNK, CHUNK), CHUNK),
        "b_spatial": 1.0 + 0.1 * jax.random.normal(ks[11], (L, GM_HEADS, CHUNK), f32),
        "w_mix_out": w(ks[12], (L, MIX_WIDTH, D_MODEL), MIX_WIDTH),
        "g_xattn": gain(ks[13], (L, D_MODEL)),
        "g_mem": gain(ks[14], (L, D_MODEL)),
        "w_xq": w(ks[15], (L, D_MODEL, D_MODEL), D_MODEL),
        "w_xk": w(ks[16], (L, D_MODEL, D_MODEL), D_MODEL),
        "w_xv": w(ks[17], (L, D_MODEL, D_MODEL), D_MODEL),
        "w_xo": w(ks[18], (L, D_MODEL, D_MODEL), D_MODEL),
        "g_ffn2": gain(ks[19], (L, D_MODEL)),
        "w_ffn2_in": w(ks[20], (L, D_MODEL, 2 * D_FF), D_MODEL),
        "w_ffn2_out": w(ks[21], (L, D_FF, D_MODEL), D_FF),
        "g_final": gain(ks[22], (D_MODEL,)),
    }

def reference(x, mem, g_ffn1, w_ffn1_in, w_ffn1_out, g_mix, w_mix_in, conv_w, conv_b,
              g_gm_v, w_spatial, b_spatial, w_mix_out, g_xattn, g_mem, w_xq, w_xk, w_xv,
              w_xo, g_ffn2, w_ffn2_in, w_ffn2_out, g_final):
    h = x
    splits = [CONV_WIDTH, 2 * CONV_WIDTH, 3 * CONV_WIDTH, 3 * CONV_WIDTH + GM_WIDTH]
    for l in range(DEPTH):
        h = h + 0.5 * _swiglu(_rmsnorm(h, g_ffn1[l]), w_ffn1_in[l], w_ffn1_out[l])

        z = _rmsnorm(h, g_mix[l]) @ w_mix_in[l]
        gate_b, gate_c, h_c, u, v = jnp.split(z, splits, axis=-1)
        y_conv = gate_b * _causal_dwconv(gate_c * h_c, conv_w[l], conv_b[l])
        y_gm = _spatial_gating(u, v, g_gm_v[l], w_spatial[l], b_spatial[l])
        h = h + jnp.concatenate([y_conv, y_gm], axis=-1) @ w_mix_out[l]

        h = h + _cross_attention(_rmsnorm(h, g_xattn[l]), _rmsnorm(mem, g_mem[l]),
                                 w_xq[l], w_xk[l], w_xv[l], w_xo[l])

        h = h + 0.5 * _swiglu(_rmsnorm(h, g_ffn2[l]), w_ffn2_in[l], w_ffn2_out[l])
    return _rmsnorm(h, g_final)


_drawn_inputs = setup_inputs


def setup_inputs(seed=0):
    import zlib

    import numpy as np

    out = dict(_drawn_inputs(seed))
    spreads = {}
    factors = {'conv_b': 8.0, 'g_xattn': 8.0, 'g_mem': 5.592, 'g_ffn2': 7.575}
    for name, (base, spread) in spreads.items():
        noise = np.random.default_rng([zlib.crc32(name.encode()), seed]).standard_normal(out[name].shape)
        drawn = base * np.exp(spread * noise) if base else spread * noise
        out[name] = __import__('jax').numpy.asarray(drawn.astype(out[name].dtype))
    for name, factor in factors.items():
        out[name] = (out[name] * factor).astype(out[name].dtype)
    return out
```

```python
from contextlib import ExitStack

import concourse.bass as bass
from concourse import mybir

ALU = mybir.AluOpType
ACT = mybir.ActivationFunctionType
AX_X = mybir.AxisListType.X
F32 = mybir.dt.float32
F32R = mybir.dt.float32r

P = 128
TOK = 2
SEQ = TOK * P
BLK = 512
GW = 2 * BLK
SETW = 4 * BLK
RAW = 4
RING = 4
EPS = 1e-6
XA_HEADS = 4


def starts(steps):
    at, n = {}, 0
    for name, k in steps:
        at[name] = n
        n += k
    return at


def build(nc, x, mem, g_ffn1, w_ffn1_in, w_ffn1_out, g_mix, w_mix_in, conv_w, conv_b, g_gm_v, w_spatial, b_spatial,
          w_mix_out, g_xattn, g_mem, w_xq, w_xk, w_xv, w_xo, g_ffn2, w_ffn2_in, w_ffn2_out, g_final, out):
    D = x.shape[2]
    KD = D // P
    FF = w_ffn1_out.shape[1]
    KF = FF // P
    FG = FF // BLK
    HEADS = w_spatial.shape[1]
    HALF = GW // P
    HD = D // XA_HEADS
    DT = HD // P
    SCALE = float(HD) ** -0.5
    assert KD % RING == 0 and KF % RING == 0 and FG % 2 == 1 and D == 2 * GW and HEADS == HALF

    groups = [(f"ffn1_in{g}", KD) for g in range(FG)] + [("ffn1_out0", KF), ("ffn1_out1", KF)]
    groups += [(n, KD) for n in ("C", "H", "B", "V", "U", "mix_out0", "mix_out1", "q0", "k0", "q1", "k1", "v0", "v1",
                                 "xo0", "xo1")]
    groups += [(f"ffn2_in{g}", KD) for g in range(FG)] + [("ffn2_out0", KF), ("ffn2_out1", KF)]
    UNIT0 = starts(groups)
    UNITS = dict(groups)
    SET = {name: i % 2 for i, (name, _) in enumerate(groups)}

    def done(group):
        return UNIT0[group] + UNITS[group]

    f1 = [(f"ffn1_in{g}", 2) for g in range(FG)]
    f2 = [(f"ffn2_in{g}", 2) for g in range(FG)]
    TURN = starts([("x0", 4), ("x1", 4)] + f1 + [("ffn1_out0", 4), ("ffn1_out1", 4), ("ws", 2), ("H", 4), ("B", 4),
                  ("U", 4), ("mix_out0", 4), ("memA", 4), ("mix_out1", 4), ("memB", 4), ("q0", 4), ("k0", 4),
                  ("p0", 2), ("q1", 4), ("k1", 4), ("p1", 2), ("xo0", 4), ("xo1", 4)] + f2)
    HI = starts([("x0", 4), ("x1", 4)] + f1 + [("ffn1_out0", 4), ("ffn1_out1", 4), ("U", 4), ("mix_out0", 4),
                ("memA", 4), ("mix_out1", 4), ("memB", 4), ("pv0", 4), ("pv1", 4), ("xo0", 4), ("xo1", 4)] + f2)
    TAKEN = starts([("x0", 4), ("x1", 4)] + f1 + [("ffn1_out0", 4), ("ffn1_out1", 4), ("ws", 2), ("U", 4),
                   ("mix_out0", 4), ("memA", 4), ("mix_out1", 4), ("memB", 4), ("q0", 4), ("k0", 4), ("p0", 2),
                   ("q1", 4), ("k1", 4), ("p1", 2), ("pv0", 4), ("pv1", 4), ("xo0", 4), ("xo1", 4)] + f2)
    STAGED = starts([(f"ffn1_in{g}", 2) for g in range(FG)] + [(n, 2) for n in (
        "ffn1_out0", "ffn1_out1", "H", "B", "U", "mix_out0", "mix_out1", "q0", "k0", "q1", "k1", "xo0", "xo1")]
        + [(f"ffn2_in{g}", 2) for g in range(FG)] + [("ffn2_out0", 2), ("ffn2_out1", 2)])
    SQUARED = starts([(n, 2) for n in ("x0", "x1", "ffn1_out0", "ffn1_out1", "mix_out0", "mix_out1", "mem0", "mem1",
                                       "xo0", "xo1", "ffn2_out0", "ffn2_out1")])
    NORM = starts([(n, 1) for n in ("x", "ffn1", "v", "mix", "mem", "xo", "final")])

    BASE = (nc.sbuf_base + 31) // 32 * 32
    KB = 1024
    place = {"at": BASE}

    def put(name, shape, dt, at=None):
        size = 4
        for s in shape[1:]:
            size *= s
        if at is None:
            at = place["at"]
            place["at"] = at + (size + 31) // 32 * 32
        return nc.alloc_sbuf_tensor_at(name, shape, dt, offset=at)

    h = put("h", [P, TOK, D], F32)
    xT_hi = put("xT_hi", [P, KD, SEQ], F32R)
    xT_lo = put("xT_lo", [P, KD, SEQ], F32R)
    raw = put("raw", [P, RAW, GW], F32)
    w_hi = put("w_hi", [P, RING, GW], F32R)
    w_lo = put("w_lo", [P, RING, GW], F32R)
    stage = put("stage", [P, TOK, GW], F32)
    scratch = put("scratch", [P, GW], F32)
    ident = put("ident", [P, P], F32)
    rows = put("rows", [P, P], F32)
    cols = put("cols", [P, P], F32)
    ssq = put("ssq", [P, 2, TOK], F32)
    rstd = put("rstd", [P, TOK], F32)
    rstd_mem = put("rstd_mem", [P, TOK], F32)
    rstd_v = put("rstd_v", [P, TOK * HEADS], F32)
    ssv = put("ssv", [P, TOK * HEADS], F32)
    small = put("small", [P, 4, TOK * HEADS], F32)
    smax = put("smax", [P, 4], F32)
    nbias = put("nbias", [P, 4], F32)
    rsum = put("rsum", [P, 4], F32)
    rinv = put("rinv", [P, 4], F32)
    extra = place["at"]
    g_v = put("g_v", [P, GW], F32, at=extra)
    ws = put("ws", [P, HEADS, P], F32, at=extra + 4 * KB)
    pT = put("pT", [P, XA_HEADS, 2, SEQ], F32, at=extra)
    g_fin = put("g_fin", [P, D], F32, at=extra)
    big = extra + 8 * KB
    hidT_hi = put("hidT_hi", [P, KF, SEQ], F32R, at=big)
    hidT_lo = put("hidT_lo", [P, KF, SEQ], F32R, at=big + KF * KB)
    yT_hi = put("yT_hi", [P, KD, SEQ], F32R, at=big)
    yT_lo = put("yT_lo", [P, KD, SEQ], F32R, at=big + 16 * KB)
    memT_hi = put("memT_hi", [P, KD, SEQ], F32R, at=big + 32 * KB)
    memT_lo = put("memT_lo", [P, KD, SEQ], F32R, at=big + 48 * KB)
    c_buf = put("c_buf", [P, TOK, GW], F32, at=big + 32 * KB)
    zT = put("zT", [P, HALF, SEQ], F32, at=big + 40 * KB)
    convT = put("convT", [P, HALF, SEQ], F32, at=big + 48 * KB)
    v_buf = put("v_buf", [P, TOK, GW], F32, at=big + 56 * KB)
    wsT = put("wsT", [P, HEADS, P], F32, at=big + 64 * KB)
    sg = put("sg", [P, TOK, GW], F32, at=big + 80 * KB)
    mem_nat = put("mem_nat", [P, TOK, D], F32, at=big + 64 * KB)
    qT = put("qT", [P, HALF, SEQ], F32, at=big + 64 * KB)
    kT = put("kT", [P, HALF, SEQ], F32, at=big + 72 * KB)
    v_mem = put("v_mem", [P, TOK, GW], F32, at=big + 80 * KB)
    assert big + 2 * KF * KB <= nc.sbuf_usable_end

    vectors = [("g_ffn1", g_ffn1[0], KD), ("g_mix", g_mix[0], KD), ("g_xattn", g_xattn[0], KD), ("g_mem", g_mem[0], KD),
               ("g_ffn2", g_ffn2[0], KD), ("conv_w", conv_w[0].rearrange("k c -> (k c)"), 3 * HALF),
               ("conv_b", conv_b[0], HALF), ("b_spatial", b_spatial[0].rearrange("h t -> (h t)"), HEADS)]
    ROW = starts([(n, k) for n, _, k in vectors])
    NROWS = sum(k for _, _, k in vectors)

    def col(name, k):
        return cols[:, ROW[name] + k:ROW[name] + k + 1]

    with ExitStack() as ctx:
        def sem(name):
            return ctx.enter_context(nc.semaphore(name))

        ps = ctx.enter_context(nc.psum_tensor("ps", [P, 2 * SETW], F32))

        def bank(s, c0, n):
            return ps[:, s * SETW + c0:s * SETW + c0 + n]

        raw_loaded = [sem(f"raw_loaded{i}") for i in range(RAW)]
        hi_ready = sem("hi_ready")
        lo_ready = sem("lo_ready")
        unit_used = sem("unit_used")
        staged = sem("staged")
        turned = sem("turned")
        hi_taken = sem("hi_taken")
        taken = sem("taken")
        silu_ready = sem("silu_ready")
        squared = sem("squared")
        ms_ready = sem("ms_ready")
        root_ready = sem("root_ready")
        rstd_ready = sem("rstd_ready")
        dve_step = sem("dve_step")
        act_step = sem("act_step")
        x_loaded = [sem("x_loaded0"), sem("x_loaded1")]
        rows_loaded = sem("rows_loaded")
        gv_loaded = sem("gv_loaded")
        ws_loaded = sem("ws_loaded")
        mem_loaded = sem("mem_loaded")
        gfin_loaded = sem("gfin_loaded")
        ident_zero = sem("ident_zero")
        ident_ready = sem("ident_ready")
        ws_masked = sem("ws_masked")
        rows_turned = sem("rows_turned")
        cols_ready = sem("cols_ready")
        c_taken = sem("c_taken")
        z_taken = sem("z_taken")
        conv_done = sem("conv_done")
        yc_product = sem("yc_product")
        yc_hi = sem("yc_hi")
        yc_ready = sem("yc_ready")
        v_squared = sem("v_squared")
        vn_ready = sem("vn_ready")
        gated = sem("gated")
        sg_ready = sem("sg_ready")
        scored = sem("scored")
        nbias_ready = sem("nbias_ready")
        exp_ready = sem("exp_ready")
        probs_ready = sem("probs_ready")
        v_taken = sem("v_taken")
        pv_done = sem("pv_done")
        out_ready = sem("out_ready")
        out_stored = sem("out_stored")

        block = ctx.enter_context(nc.Block())

        def ffn_in_src(w, col0):
            v = w[0].rearrange("(k p) (s n) -> k p s n", p=P, s=2)
            return lambda k: v[k][:, :, bass.ds(col0, BLK)]

        def cols_src(w, col0):
            v = w[0].rearrange("(k p) n -> k p n", p=P)
            return lambda k: v[k][:, col0:col0 + GW]

        @block.sync
        def _(sp):
            def load_units(src, unit0, n):
                for k in range(n):
                    dst = raw[:, k % RAW, :]
                    if len(src(k).shape) == 3:
                        dst = dst.rearrange("p (s n) -> p s n", s=2)
                    if not (isinstance(unit0, int) and unit0 + k < RAW):
                        sp.wait_ge(lo_ready, unit0 + (k - RAW + 1))
                    sp.dma_start(dst, src(k)).then_inc(raw_loaded[k % RAW], 16)

            def load_ffn_in(f, w):
                u0 = UNIT0[f"ffn{f}_in0"]
                load_units(ffn_in_src(w, 0), u0, KD)
                with sp.Fori(0, FG // 2) as i:
                    for j in range(2):
                        load_units(ffn_in_src(w, i * GW + (1 + j) * BLK), i * (2 * KD) + (u0 + (1 + j) * KD), KD)

            def load_pair(name, w, n):
                for c in range(2):
                    load_units(cols_src(w, c * GW), UNIT0[f"{name}{c}"], n)

            xv = x[0].rearrange("(t p) n -> p t n", p=P)
            for c in range(2):
                sp.dma_start(h[:, :, c * GW:(c + 1) * GW], xv[:, :, c * GW:(c + 1) * GW]).then_inc(x_loaded[c], 16)
            load_ffn_in(1, w_ffn1_in)
            load_pair("ffn1_out", w_ffn1_out, KF)
            for name, c in (("C", 1), ("H", 2), ("B", 0), ("V", 4), ("U", 3)):
                load_units(cols_src(w_mix_in, c * GW), UNIT0[name], KD)
            sp.wait_ge(gated, 4)
            sp.dma_start(mem_nat[:, :, :], mem[0].rearrange("(t p) n -> p t n", p=P)).then_inc(mem_loaded, 16)
            load_pair("mix_out", w_mix_out, KD)
            for c in range(2):
                load_units(cols_src(w_xq, c * GW), UNIT0[f"q{c}"], KD)
                load_units(cols_src(w_xk, c * GW), UNIT0[f"k{c}"], KD)
            load_pair("v", w_xv, KD)
            load_pair("xo", w_xo, KD)
            sp.wait_ge(pv_done, 8)
            sp.dma_start(g_fin[:, :], g_final.partition_broadcast(P)).then_inc(gfin_loaded, 16)
            load_ffn_in(2, w_ffn2_in)
            load_pair("ffn2_out", w_ffn2_out, KF)
            ov = out[0].rearrange("(t p) n -> p t n", p=P)
            for t in range(TOK):
                sp.wait_ge(out_ready, t + 1)
                sp.dma_start(ov[:, t, :], h[:, t, :]).then_inc(out_stored, 16)
            sp.wait_ge(out_stored, 16 * TOK)

        @block.gpsimd
        def _(pool):
            pool.memset(ident[:, :], 0.0).then_inc(ident_zero, 1)
            pool.wait_ge(ident_zero, 1)
            pool.affine_select(out=ident[:, :], in_=ident[:, :], compare_op=ALU.not_equal, fill=1.0, base=0,
                               pattern=[[-1, P]], channel_multiplier=1).then_inc(ident_ready, 1)
            pool.wait_ge(ws_loaded, 16)
            pool.affine_select(out=ws[:, :, :], in_=ws[:, :, :], compare_op=ALU.is_ge, fill=0.0, base=0,
                               pattern=[[0, HEADS], [-1, P]], channel_multiplier=1).then_inc(ws_masked, 1)

        @block.scalar
        def _(act):
            def hi_units(unit0, k0, k1):
                for k in range(k0, k1):
                    act.wait_ge(raw_loaded[k % RAW], unit0 * (16 // RAW) + 16 * (k // RAW + 1))
                    if not (isinstance(unit0, int) and unit0 + k < RING):
                        act.wait_ge(unit_used, unit0 + (k - RING + 1))
                    nc.scalar.activation(w_hi[:, k % RING, :], raw[:, k % RAW, :], ACT.Copy).then_inc(hi_ready, 1)

            def hi_scaled(dst, k0, g, s, name):
                for b in range(4):
                    act.wait_ge(turned, TURN[name] + b + 1)
                    for j in range(2):
                        k = 2 * b + j
                        ins = nc.scalar.activation(dst[:, k0 + k, :], bank(s, k * SEQ, SEQ), ACT.Copy, scale=col(g, k0 + k))
                    ins.then_inc(hi_taken, 1)

            def hi_plain(dst, k0, s, banks, ready, first):
                for b in range(banks):
                    act.wait_ge(ready, first + b + 1)
                    nc.scalar.activation(dst[:, bass.ds(k0 + 2 * b, 2), :].rearrange("p k t -> p (k t)"),
                                         bank(s, b * BLK, BLK), ACT.Copy).then_inc(hi_taken, 1)

            def squares(src, c, name):
                for t in range(TOK):
                    if SQUARED[name] + t > 0:
                        act.wait_ge(squared, SQUARED[name] + t)
                    nc.scalar.activation(scratch[:, :], src[:, t, c * GW:(c + 1) * GW], ACT.Square,
                                         accum_out=ssq[:, c, t:t + 1]).then_inc(squared, 1)

            def root(norm, n):
                act.wait_ge(ms_ready, NORM[norm] + 1)
                nc.scalar.activation(small[:, 1, 0:n], small[:, 0, 0:n], ACT.Sqrt).then_inc(root_ready, 1)

            def silu(s, used):
                act.wait_ge(unit_used, used)
                for t in range(TOK):
                    nc.scalar.activation(scratch[:, t * BLK:(t + 1) * BLK], bank(s, t * GW, BLK), ACT.Silu,
                                         scale=rstd[:, t:t + 1]).then_inc(silu_ready, 1)

            def resid(name, c, dst, g, first, half):
                hi_units(first, 0, 4)
                act.wait_ge(staged, STAGED[name] + TOK)
                squares(h, c, name)
                hi_units(first, 4, 8)
                hi_scaled(dst, c * HALF, g, half, name)

            def ffn_in(f, norm):
                u0 = UNIT0[f"ffn{f}_in0"]
                act.wait_ge(rstd_ready, NORM[norm] + 1)
                with act.Fori(0, FG // 2) as i:
                    for j in range(2):
                        unit0 = i * (2 * KD) + (u0 + (1 + j) * KD)
                        hi_units(unit0, 0, 4)
                        silu(j, unit0)
                        hi_units(unit0, 4, 8)
                        hi_plain(hidT_hi, i * 8 + 4 * j, j, 2, turned, i * 4 + (TURN[f"ffn{f}_in0"] + 2 * j))
                        hi_units(unit0, 8, KD)

            def ffn_out(f):
                last = f"ffn{f}_in{FG - 1}"
                u0 = UNIT0[f"ffn{f}_out0"]
                hi_units(u0, 0, 4)
                silu(SET[last], u0)
                hi_units(u0, 4, 8)
                hi_plain(hidT_hi, 4 * (FG - 1), SET[last], 2, turned, TURN[last])
                hi_units(u0, 8, KF)

            for i, (name, v, k) in enumerate(vectors):
                r = ROW[name]
                act.dma_start(rows[r:r + k, :], v.rearrange("(r c) -> r c", c=P)).then_inc(rows_loaded, 16)
            act.dma_start(ws[:, :, :], w_spatial[0].rearrange("h t s -> t h s")).then_inc(ws_loaded, 16)
            act.dma_start(g_v[:, :], g_gm_v[0].partition_broadcast(P)).then_inc(gv_loaded, 16)

            act.wait_ge(cols_ready, 1)
            hi_scaled(xT_hi, 0, "g_ffn1", 0, "x0")
            hi_units(0, 0, 2)
            hi_scaled(xT_hi, HALF, "g_ffn1", 1, "x1")
            hi_units(0, 2, 4)
            for c in range(2):
                act.wait_ge(x_loaded[c], 16)
                squares(h, c, f"x{c}")
            hi_units(0, 4, 8)
            root("x", TOK)
            hi_units(0, 8, KD)
            ffn_in(1, "x")
            ffn_out(1)
            u = UNIT0["ffn1_out1"]
            resid("ffn1_out0", 0, xT_hi, "g_mix", u, SET["ffn1_out0"])
            hi_units(u, 8, KF)
            u = UNIT0["C"]
            resid("ffn1_out1", 1, xT_hi, "g_mix", u, SET["ffn1_out1"])
            root("ffn1", TOK)
            hi_units(u, 8, KD)
            u = UNIT0["H"]
            hi_units(u, 0, 4)
            act.wait_ge(unit_used, done("C"))
            act.wait_ge(rstd_ready, NORM["ffn1"] + 1)
            for t in range(TOK):
                nc.scalar.activation(c_buf[:, t, :], bank(SET["C"], t * GW, GW), ACT.Copy,
                                     scale=rstd[:, t:t + 1]).then_inc(c_taken, 1)
            hi_units(u, 4, KD)
            u = UNIT0["B"]
            hi_units(u, 0, 8)
            for b in range(4):
                act.wait_ge(turned, TURN["H"] + b + 1)
                nc.scalar.activation(zT[:, 2 * b:2 * b + 2, :].rearrange("p k t -> p (k t)"), bank(SET["H"], b * BLK, BLK),
                                     ACT.Copy)
                for k in (2 * b, 2 * b + 1):
                    nc.scalar.activation(convT[:, k, :], bank(SET["H"], k * SEQ, SEQ), ACT.Identity,
                                         scale=col("conv_w", 2 * HALF + k), bias=col("conv_b", k)).then_inc(z_taken, 1)
            hi_units(u, 8, KD)
            u = UNIT0["V"]
            hi_units(u, 0, 9)
            act.wait_ge(yc_product, 1)
            nc.scalar.activation(yT_hi[:, 0:HALF, :], convT[:, :, :], ACT.Copy).then_inc(yc_hi, 1)
            hi_units(u, 9, KD)
            u = UNIT0["U"]
            hi_units(u, 0, 4)
            act.wait_ge(unit_used, done("V"))
            for t in range(TOK):
                nc.scalar.activation(v_buf[:, t, :], bank(SET["V"], t * GW, GW), ACT.Copy,
                                     scale=rstd[:, t:t + 1]).then_inc(act_step, 1)
            act.wait_ge(act_step, TOK)
            act.wait_ge(staged, STAGED["H"] + TOK)
            nc.scalar.activation(c_buf[:, :, :], v_buf[:, :, :], ACT.Square).then_inc(v_squared, 1)
            hi_units(u, 4, 7)
            root("v", TOK * HEADS)
            hi_units(u, 7, 14)
            for hd in range(HEADS):
                if hd % 2 == 0:
                    act.wait_ge(gated, hd // 2 + 1)
                nc.scalar.activation(sg[:, :, hd * P:(hd + 1) * P],
                                     bank(SET["V"], hd * SEQ, SEQ).rearrange("p (t c) -> p t c", t=TOK), ACT.Identity,
                                     bias=col("b_spatial", hd)).then_inc(sg_ready, 1)
            hi_units(u, 14, KD)
            u = UNIT0["mix_out0"]
            hi_units(u, 0, 8)
            hi_plain(yT_hi, HALF, SET["U"], 4, turned, TURN["U"])
            hi_units(u, 8, KD)
            u = UNIT0["mix_out1"]
            resid("mix_out0", 0, xT_hi, "g_xattn", u, SET["mix_out0"])
            hi_units(u, 8, 13)
            hi_scaled(memT_hi, 0, "g_mem", SET["mix_out0"], "memA")
            hi_units(u, 13, KD)
            u = UNIT0["q0"]
            resid("mix_out1", 1, xT_hi, "g_xattn", u, SET["mix_out1"])
            root("mix", TOK)
            hi_units(u, 8, 13)
            hi_scaled(memT_hi, HALF, "g_mem", SET["mix_out1"], "memB")
            hi_units(u, 13, KD)
            u = UNIT0["k0"]
            hi_units(u, 0, 4)
            for c in range(2):
                squares(mem_nat, c, f"mem{c}")
            hi_units(u, 4, 8)
            root("mem", TOK)
            hi_units(u, 8, KD)

            def exps(pair):
                act.wait_ge(nbias_ready, pair + 1)
                for j in range(4):
                    nc.scalar.activation(scratch[:, j * SEQ:(j + 1) * SEQ], bank(1, j * SEQ, SEQ), ACT.Exp,
                                         bias=nbias[:, j:j + 1], scale=SCALE, accum_out=rsum[:, j:j + 1]
                                         ).then_inc(exp_ready, 1)

            def take_v(pair):
                name = f"v{pair}"
                act.wait_ge(unit_used, done(name))
                for t in range(TOK):
                    nc.scalar.activation(v_mem[:, t, :], bank(SET[name], t * GW, GW), ACT.Copy,
                                         scale=rstd_mem[:, t:t + 1]).then_inc(v_taken, 1)

            u = UNIT0["q1"]
            hi_units(u, 0, 10)
            exps(0)
            hi_units(u, 10, KD)
            hi_units(UNIT0["k1"], 0, KD)
            u = UNIT0["v0"]
            hi_units(u, 0, 10)
            exps(1)
            hi_units(u, 10, KD)
            for pair, name in enumerate(("v1", "xo0")):
                u = UNIT0[name]
                hi_units(u, 0, 4)
                act.wait_ge(rstd_ready, NORM["mem"] + 1)
                take_v(pair)
                hi_units(u, 4, 9)
                hi_plain(yT_hi, pair * HALF, SET[f"v{pair}"], 4, pv_done, 4 * pair)
                hi_units(u, 9, KD)
            u = UNIT0["xo1"]
            resid("xo0", 0, xT_hi, "g_ffn2", u, SET["xo0"])
            hi_units(u, 8, KD)
            u = UNIT0["ffn2_in0"]
            resid("xo1", 1, xT_hi, "g_ffn2", u, SET["xo1"])
            root("xo", TOK)
            hi_units(u, 8, KD)
            ffn_in(2, "xo")
            ffn_out(2)
            u = UNIT0["ffn2_out1"]
            hi_units(u, 0, 4)
            act.wait_ge(staged, STAGED["ffn2_out0"] + TOK)
            squares(h, 0, "ffn2_out0")
            hi_units(u, 4, KF)
            act.wait_ge(staged, STAGED["ffn2_out1"] + TOK)
            squares(h, 1, "ffn2_out1")
            root("final", TOK)

        @block.vector
        def _(dve):
            steps = [0]

            def chain(ins):
                ins.then_inc(dve_step, 1)
                steps[0] += 1
                dve.wait_ge(dve_step, steps[0])

            def lo_units(unit0, k0, k1):
                for k in range(k0, k1):
                    dve.wait_ge(hi_ready, unit0 + (k + 1))
                    nc.vector.tensor_tensor(w_lo[:, k % RING, :], raw[:, k % RAW, :], w_hi[:, k % RING, :].bitcast(F32),
                                            ALU.subtract).then_inc(lo_ready, 1)

            def lo_scaled(dst, hi, k0, g, s, name):
                for b in range(4):
                    dve.wait_ge(hi_taken, HI[name] + b + 1)
                    for j in range(2):
                        k = 2 * b + j
                        ins = nc.vector.scalar_tensor_tensor(out=dst[:, k0 + k, :], in0=bank(s, k * SEQ, SEQ),
                                                             scalar=col(g, k0 + k), in1=hi[:, k0 + k, :].bitcast(F32),
                                                             op0=ALU.mult, op1=ALU.subtract)
                    ins.then_inc(taken, 1)

            def lo_plain(dst, hi, k0, s, banks, first):
                for b in range(banks):
                    dve.wait_ge(hi_taken, first + b + 1)
                    nc.vector.tensor_tensor(dst[:, bass.ds(k0 + 2 * b, 2), :].rearrange("p k t -> p (k t)"),
                                            bank(s, b * BLK, BLK),
                                            hi[:, bass.ds(k0 + 2 * b, 2), :].rearrange("p k t -> p (k t)").bitcast(F32),
                                            ALU.subtract).then_inc(taken, 1)

            def copy_turned(dst, s, banks, b0, name):
                for b in range(banks):
                    dve.wait_ge(turned, TURN[name] + b + 1)
                    nc.vector.tensor_copy(dst[:, b * BLK:(b + 1) * BLK], bank(s, (b0 + b) * BLK, BLK)).then_inc(taken, 1)

            def norm(name, total, n, count, res):
                ms, rt, inv, t = (small[:, i, 0:n] for i in range(4))
                if total is None:
                    chain(nc.vector.tensor_tensor(t, ssq[:, 0, :], ssq[:, 1, :], ALU.add))
                    total = t
                nc.vector.tensor_scalar(ms, total, 1.0 / count, EPS, ALU.mult, ALU.add).then_inc(ms_ready, 1)
                dve.wait_ge(root_ready, NORM[name] + 1)
                chain(nc.vector.reciprocal(inv, rt))
                chain(nc.vector.tensor_tensor(t, inv, inv, ALU.mult))
                chain(nc.vector.tensor_tensor(t, t, ms, ALU.mult))
                chain(nc.vector.tensor_scalar(t, t, -0.5, 1.5, ALU.mult, ALU.add))
                nc.vector.tensor_tensor(res, inv, t, ALU.mult).then_inc(rstd_ready, 1)
                dve.wait_ge(rstd_ready, NORM[name] + 1)

            def add_resid(name, c, coef):
                dve.wait_ge(unit_used, done(name))
                for t in range(TOK):
                    hs = h[:, t, c * GW:(c + 1) * GW]
                    nc.vector.scalar_tensor_tensor(out=hs, in0=bank(SET[name], t * GW, GW), scalar=coef, in1=hs,
                                                   op0=ALU.mult, op1=ALU.add).then_inc(staged, 1)

            def resid(name, c, coef, g, first):
                lo_units(first, 0, 4)
                add_resid(name, c, coef)
                lo_units(first, 4, 8)
                lo_scaled(xT_lo, xT_hi, c * HALF, g, SET[name], name)

            def gate(s, silus):
                for t in range(TOK):
                    dve.wait_ge(silu_ready, silus + t + 1)
                    nc.vector.scalar_tensor_tensor(out=stage[:, t, 0:BLK], in0=bank(s, t * GW + BLK, BLK),
                                                   scalar=rstd[:, t:t + 1], in1=scratch[:, t * BLK:(t + 1) * BLK],
                                                   op0=ALU.mult, op1=ALU.mult).then_inc(staged, 1)

            def ffn_in(f):
                u0 = UNIT0[f"ffn{f}_in0"]
                s0 = (f - 1) * 2 * FG
                with dve.Fori(0, FG // 2) as i:
                    for j in range(2):
                        unit0 = i * (2 * KD) + (u0 + (1 + j) * KD)
                        lo_units(unit0, 0, 4)
                        gate(j, i * 4 + (s0 + 2 * j))
                        lo_units(unit0, 4, 8)
                        lo_plain(hidT_lo, hidT_hi, i * 8 + 4 * j, j, 2, i * 4 + (HI[f"ffn{f}_in0"] + 2 * j))
                        lo_units(unit0, 8, KD)

            def ffn_out(f):
                last = f"ffn{f}_in{FG - 1}"
                u0 = UNIT0[f"ffn{f}_out0"]
                lo_units(u0, 0, 4)
                gate(SET[last], (f - 1) * 2 * FG + 2 * (FG - 1))
                lo_units(u0, 4, 8)
                lo_plain(hidT_lo, hidT_hi, 4 * (FG - 1), SET[last], 2, HI[last])
                lo_units(u0, 8, KF)

            def scaled(name, scale):
                dve.wait_ge(unit_used, done(name))
                for t in range(TOK):
                    nc.vector.tensor_scalar(stage[:, t, :], bank(SET[name], t * GW, GW), scale[:, t:t + 1], None,
                                            ALU.mult).then_inc(staged, 1)

            dve.wait_ge(rows_turned, 1)
            nc.vector.tensor_copy(cols[:, 0:NROWS], ps[:, SETW:SETW + NROWS]).then_inc(cols_ready, 1)
            dve.wait_ge(cols_ready, 1)
            lo_scaled(xT_lo, xT_hi, 0, "g_ffn1", 0, "x0")
            lo_units(0, 0, 2)
            lo_scaled(xT_lo, xT_hi, HALF, "g_ffn1", 1, "x1")
            lo_units(0, 2, 8)
            dve.wait_ge(squared, SQUARED["x1"] + 2)
            norm("x", None, TOK, D, rstd[:, :])
            lo_units(0, 8, KD)
            ffn_in(1)
            ffn_out(1)
            u = UNIT0["ffn1_out1"]
            resid("ffn1_out0", 0, 0.5, "g_mix", u)
            lo_units(u, 8, KF)
            u = UNIT0["C"]
            resid("ffn1_out1", 1, 0.5, "g_mix", u)
            dve.wait_ge(squared, SQUARED["ffn1_out1"] + 2)
            norm("ffn1", None, TOK, D, rstd[:, :])
            lo_units(u, 8, 13)
            copy_turned(wsT[:, :, :].rearrange("s h t -> s (h t)"), SET["ffn1_out1"], 2, 0, "ws")
            lo_units(u, 13, KD)
            lo_units(UNIT0["H"], 0, KD)
            u = UNIT0["B"]
            lo_units(u, 0, 4)
            dve.wait_ge(unit_used, done("H"))
            for t in range(TOK):
                dve.wait_ge(c_taken, t + 1)
                nc.vector.scalar_tensor_tensor(out=stage[:, t, :], in0=bank(SET["H"], t * GW, GW), scalar=rstd[:, t:t + 1],
                                               in1=c_buf[:, t, :], op0=ALU.mult, op1=ALU.mult).then_inc(staged, 1)
            lo_units(u, 4, 12)
            dve.wait_ge(z_taken, HALF)
            for shift in (1, 2):
                for k in range(HALF):
                    y = convT[:, k, shift:SEQ]
                    ins = nc.vector.scalar_tensor_tensor(out=y, in0=zT[:, k, 0:SEQ - shift],
                                                         scalar=col("conv_w", (2 - shift) * HALF + k), in1=y,
                                                         op0=ALU.mult, op1=ALU.add)
                    ins.then_inc(conv_done, 1)
                dve.wait_ge(conv_done, HALF * shift)
            lo_units(u, 12, KD)
            u = UNIT0["V"]
            lo_units(u, 0, 4)
            scaled("B", rstd)
            lo_units(u, 4, 8)
            cv = convT[:, :, :].rearrange("p k t -> p (k t)")
            dve.wait_ge(turned, TURN["B"] + 4)
            nc.vector.tensor_tensor(cv, cv, bank(SET["B"], 0, SETW), ALU.mult).then_inc(yc_product, 1)
            lo_units(u, 8, 10)
            dve.wait_ge(yc_product, 1)
            dve.wait_ge(yc_hi, 1)
            nc.vector.tensor_tensor(yT_lo[:, 0:HALF, :], convT[:, :, :], yT_hi[:, 0:HALF, :].bitcast(F32),
                                    ALU.subtract).then_inc(yc_ready, 1)
            lo_units(u, 10, KD)
            u = UNIT0["U"]
            lo_units(u, 0, 6)
            dve.wait_ge(v_squared, 1)
            chain(nc.vector.tensor_reduce(ssv[:, :], c_buf[:, :, :].rearrange("p t (h c) -> p (t h) c", c=P), AX_X, ALU.add))
            norm("v", ssv[:, :], TOK * HEADS, P, rstd_v[:, :])
            vv = v_buf[:, :, :].rearrange("p t (h c) -> p (t h) c", c=P)
            chain(nc.vector.tensor_tensor(vv, vv, rstd_v[:, :].unsqueeze(2).to_broadcast([P, TOK * HEADS, P]), ALU.mult))
            lo_units(u, 6, 8)
            dve.wait_ge(gv_loaded, 16)
            for t in range(TOK):
                nc.vector.tensor_tensor(v_buf[:, t, :], v_buf[:, t, :], g_v[:, :], ALU.mult).then_inc(vn_ready, 1)
            lo_units(u, 8, KD)
            u = UNIT0["mix_out0"]
            lo_units(u, 0, 4)
            dve.wait_ge(unit_used, done("U"))
            dve.wait_ge(sg_ready, HEADS)
            for t in range(TOK):
                nc.vector.scalar_tensor_tensor(out=stage[:, t, :], in0=bank(SET["U"], t * GW, GW), scalar=rstd[:, t:t + 1],
                                               in1=sg[:, t, :], op0=ALU.mult, op1=ALU.mult).then_inc(staged, 1)
            lo_units(u, 4, 8)
            lo_plain(yT_lo, yT_hi, HALF, SET["U"], 4, HI["U"])
            lo_units(u, 8, KD)
            u = UNIT0["mix_out1"]
            resid("mix_out0", 0, 1.0, "g_xattn", u)
            lo_units(u, 8, 13)
            lo_scaled(memT_lo, memT_hi, 0, "g_mem", SET["mix_out0"], "memA")
            lo_units(u, 13, KD)
            u = UNIT0["q0"]
            resid("mix_out1", 1, 1.0, "g_xattn", u)
            dve.wait_ge(squared, SQUARED["mix_out1"] + 2)
            norm("mix", None, TOK, D, rstd[:, :])
            lo_units(u, 8, 13)
            lo_scaled(memT_lo, memT_hi, HALF, "g_mem", SET["mix_out1"], "memB")
            lo_units(u, 13, KD)

            def turned_qk(name, scale, dst, u):
                lo_units(u, 0, 4)
                scaled(name, scale)
                lo_units(u, 4, 8)
                dve.wait_ge(squared, SQUARED["mem1"] + 2)
                copy_turned(dst[:, :, :].rearrange("p k t -> p (k t)"), SET[name], 4, 0, name)

            def softmax(pair):
                dve.wait_ge(scored, pair + 1)
                chain(nc.vector.tensor_reduce(smax[:, :], bank(1, 0, 2 * BLK).rearrange("p (j m) -> p j m", j=4), AX_X, ALU.max))
                nc.vector.tensor_scalar(nbias[:, :], smax[:, :], -SCALE, None, ALU.mult).then_inc(nbias_ready, 1)
                dve.wait_ge(exp_ready, 4 * (pair + 1))
                chain(nc.vector.reciprocal(rinv[:, :], rsum[:, :]))
                pv = scratch[:, :].rearrange("p (j m) -> p j m", j=4)
                nc.vector.tensor_tensor(pv, pv, rinv[:, :].unsqueeze(2).to_broadcast([P, 4, SEQ]),
                                        ALU.mult).then_inc(probs_ready, 1)

            u = UNIT0["k0"]
            turned_qk("q0", rstd, qT, u)
            norm("mem", None, TOK, D, rstd_mem[:, :])
            lo_units(u, 8, KD)
            for pair, (kname, running) in enumerate((("k0", "q1"), ("k1", "v0"))):
                u = UNIT0[running]
                turned_qk(kname, rstd_mem, kT, u)
                lo_units(u, 8, 10)
                softmax(pair)
                lo_units(u, 10, 14)
                copy_turned(pT[:, 2 * pair:2 * pair + 2, :, :].rearrange("p h m t -> p (h m t)"), 1, 2, 2, f"p{pair}")
                lo_units(u, 14, KD)
                if pair == 0:
                    u = UNIT0["k1"]
                    turned_qk("q1", rstd, qT, u)
                    lo_units(u, 8, KD)
            for pair, running in enumerate(("v1", "xo0")):
                u = UNIT0[running]
                lo_units(u, 0, 9)
                lo_plain(yT_lo, yT_hi, pair * HALF, SET[f"v{pair}"], 4, HI[f"pv{pair}"])
                lo_units(u, 9, KD)
            u = UNIT0["xo1"]
            resid("xo0", 0, 1.0, "g_ffn2", u)
            lo_units(u, 8, KD)
            u = UNIT0["ffn2_in0"]
            resid("xo1", 1, 1.0, "g_ffn2", u)
            dve.wait_ge(squared, SQUARED["xo1"] + 2)
            norm("xo", None, TOK, D, rstd[:, :])
            lo_units(u, 8, KD)
            ffn_in(2)
            ffn_out(2)
            u = UNIT0["ffn2_out1"]
            lo_units(u, 0, 4)
            add_resid("ffn2_out0", 0, 0.5)
            lo_units(u, 4, KF)
            add_resid("ffn2_out1", 1, 0.5)
            dve.wait_ge(squared, SQUARED["ffn2_out1"] + 2)
            norm("final", None, TOK, D, rstd[:, :])
            dve.wait_ge(gfin_loaded, 16)
            dve.wait_ge(staged, STAGED["ffn2_out1"] + TOK)
            for t in range(TOK):
                nc.vector.scalar_tensor_tensor(out=h[:, t, :], in0=h[:, t, :], scalar=rstd[:, t:t + 1], in1=g_fin[:, :],
                                               op0=ALU.mult, op1=ALU.mult).then_inc(out_ready, 1)

        @block.tensor
        def _(pe):
            def mul_units(unit0, n, k0, k1, T_hi, T_lo, s):
                for k in range(k0, k1):
                    pe.wait_ge(lo_ready, unit0 + (k + 1))
                    for t in range(TOK):
                        for xs, ws_ in ((T_hi, w_hi), (T_hi, w_lo), (T_lo, w_hi)):
                            for b in range(2):
                                ins = nc.tensor.matmul(bank(s, t * GW + b * BLK, BLK), xs[:, k, t * P:(t + 1) * P],
                                                       ws_[:, k % RING, b * BLK:(b + 1) * BLK],
                                                       start=(k == 0 and xs is T_hi and ws_ is w_hi),
                                                       stop=(k == n - 1 and xs is T_lo))
                    ins.then_inc(unit_used, 1)

            def turn(src, s, tiles, b0=0):
                for k in range(tiles):
                    for t in range(TOK):
                        ins = nc.tensor.transpose(bank(s, b0 * BLK + k * SEQ + t * P, P), src(k, t), ident[:, :])
                    if k % 2 == 1:
                        ins.then_inc(turned, 1)

            def from_stage(k, t):
                return stage[:, t, k * P:(k + 1) * P]

            def from_half(a, c):
                return lambda k, t: a[:, t, c * GW + k * P:c * GW + (k + 1) * P]

            def group(name, T_hi, T_lo, k0, k1):
                mul_units(UNIT0[name], UNITS[name], k0, k1, T_hi, T_lo, SET[name])

            def ffn_in(f):
                u0 = UNIT0[f"ffn{f}_in0"]
                with pe.Fori(0, FG // 2) as i:
                    for j in range(2):
                        unit0 = i * (2 * KD) + (u0 + (1 + j) * KD)
                        s = (1 + j) % 2
                        if j == 0:
                            pe.wait_ge(taken, i * 4 + TAKEN[f"ffn{f}_in0"])
                        else:
                            pe.wait_ge(taken, i * 4 + (TAKEN[f"ffn{f}_in0"] + 2))
                        mul_units(unit0, KD, 0, 4, xT_hi, xT_lo, s)
                        pe.wait_ge(staged, i * 4 + (STAGED[f"ffn{f}_in0"] + 2 * j + 2))
                        turn(from_stage, j, 4)
                        mul_units(unit0, KD, 4, KD, xT_hi, xT_lo, s)

            def ffn_out(f):
                last = f"ffn{f}_in{FG - 1}"
                a, b = f"ffn{f}_out0", f"ffn{f}_out1"
                pe.wait_ge(taken, TAKEN[last])
                group(a, hidT_hi, hidT_lo, 0, 4)
                pe.wait_ge(staged, STAGED[last] + TOK)
                turn(from_stage, SET[last], 4)
                group(a, hidT_hi, hidT_lo, 4, KF - 4)
                pe.wait_ge(taken, TAKEN[last] + 2)
                group(a, hidT_hi, hidT_lo, KF - 4, KF)
                group(b, hidT_hi, hidT_lo, 0, 4)
                pe.wait_ge(staged, STAGED[a] + TOK)
                if f == 1:
                    turn(from_half(h, 0), SET[a], HALF)
                group(b, hidT_hi, hidT_lo, 4, KF)

            def resid(name, c, first, T_hi, T_lo, before):
                pe.wait_ge(taken, before)
                group(first, T_hi, T_lo, 0, 4)
                pe.wait_ge(staged, STAGED[name] + TOK)
                turn(from_half(h, c), SET[name], HALF)
                group(first, T_hi, T_lo, 4, 8)

            pe.wait_ge(ident_ready, 1)
            pe.wait_ge(rows_loaded, 16 * len(vectors))
            nc.tensor.transpose(ps[:, SETW:SETW + NROWS], rows[0:NROWS, :], ident[0:NROWS, 0:NROWS]).then_inc(rows_turned, 1)
            for c in range(2):
                pe.wait_ge(x_loaded[c], 16)
                if c == 1:
                    pe.wait_ge(cols_ready, 1)
                turn(from_half(h, c), c, HALF)
            pe.wait_ge(taken, TAKEN["x0"] + 4)
            group("ffn1_in0", xT_hi, xT_lo, 0, 8)
            pe.wait_ge(taken, TAKEN["x1"] + 4)
            group("ffn1_in0", xT_hi, xT_lo, 8, KD)
            ffn_in(1)
            ffn_out(1)
            resid("ffn1_out1", 1, "C", xT_hi, xT_lo, TAKEN["ffn1_out0"] + 4)
            pe.wait_ge(taken, TAKEN["ffn1_out1"] + 4)
            group("C", xT_hi, xT_lo, 8, 9)
            pe.wait_ge(ws_masked, 1)
            for hd in range(HEADS):
                ins = nc.tensor.transpose(bank(SET["ffn1_out1"], hd * P, P), ws[:, hd, :], ident[:, :])
                if hd % 4 == 3:
                    ins.then_inc(turned, 1)
            group("C", xT_hi, xT_lo, 9, KD)
            pe.wait_ge(taken, TAKEN["ws"] + 2)
            group("H", xT_hi, xT_lo, 0, KD)
            pe.wait_ge(c_taken, TOK)
            group("B", xT_hi, xT_lo, 0, 4)
            pe.wait_ge(staged, STAGED["H"] + TOK)
            turn(from_stage, SET["H"], HALF)
            group("B", xT_hi, xT_lo, 4, KD)
            pe.wait_ge(z_taken, HALF)
            group("V", xT_hi, xT_lo, 0, 4)
            pe.wait_ge(staged, STAGED["B"] + TOK)
            turn(from_stage, SET["B"], HALF)
            group("V", xT_hi, xT_lo, 4, KD)
            pe.wait_ge(yc_product, 1)
            group("U", xT_hi, xT_lo, 0, 10)
            pe.wait_ge(vn_ready, TOK)
            for hd in range(HEADS):
                ins = nc.tensor.matmul(bank(SET["V"], hd * SEQ, SEQ), wsT[:, hd, :], v_buf[:, :, hd * P:(hd + 1) * P],
                                       start=True, stop=True)
                if hd % 2 == 1:
                    ins.then_inc(gated, 1)
            group("U", xT_hi, xT_lo, 10, KD)
            pe.wait_ge(sg_ready, HEADS)
            pe.wait_ge(yc_ready, 1)
            group("mix_out0", yT_hi, yT_lo, 0, 4)
            pe.wait_ge(staged, STAGED["U"] + TOK)
            turn(from_stage, SET["U"], HALF)
            group("mix_out0", yT_hi, yT_lo, 4, 8)
            pe.wait_ge(taken, TAKEN["U"] + 4)
            group("mix_out0", yT_hi, yT_lo, 8, KD)
            resid("mix_out0", 0, "mix_out1", yT_hi, yT_lo, TAKEN["U"] + 4)
            group("mix_out1", yT_hi, yT_lo, 8, 9)
            pe.wait_ge(taken, TAKEN["mix_out0"] + 4)
            pe.wait_ge(mem_loaded, 16)
            turn(from_half(mem_nat, 0), SET["mix_out0"], HALF)
            group("mix_out1", yT_hi, yT_lo, 9, KD)
            resid("mix_out1", 1, "q0", xT_hi, xT_lo, TAKEN["memA"] + 4)
            pe.wait_ge(taken, TAKEN["mix_out1"] + 4)
            group("q0", xT_hi, xT_lo, 8, 9)
            turn(from_half(mem_nat, 1), SET["mix_out1"], HALF)
            group("q0", xT_hi, xT_lo, 9, KD)

            def turned_group(name, T_hi, T_lo, before, running, k1):
                pe.wait_ge(taken, before)
                group(running, T_hi, T_lo, 0, 4)
                pe.wait_ge(staged, STAGED[name] + TOK)
                turn(from_stage, SET[name], HALF)
                group(running, T_hi, T_lo, 4, k1)

            def scores(pair):
                pe.wait_ge(taken, TAKEN[f"k{pair}"] + 4)
                for j in range(4):
                    for d in range(DT):
                        k = (j // 2) * DT + d
                        ins = nc.tensor.matmul(bank(1, j * SEQ, SEQ), qT[:, k, (j % 2) * P:(j % 2 + 1) * P], kT[:, k, :],
                                               start=(d == 0), stop=(d == DT - 1))
                ins.then_inc(scored, 1)

            def turn_probs(pair):
                pe.wait_ge(probs_ready, pair + 1)
                for hd in range(2):
                    for m in range(2):
                        for t in range(TOK):
                            ins = nc.tensor.transpose(bank(1, 2 * BLK + (hd * 2 + m) * SEQ + t * P, P),
                                                      scratch[:, (hd * 2 + t) * SEQ + m * P:(hd * 2 + t) * SEQ + (m + 1) * P],
                                                      ident[:, :])
                    ins.then_inc(turned, 1)

            def attend(pair):
                pe.wait_ge(v_taken, TOK * (pair + 1))
                pe.wait_ge(taken, TAKEN[f"p{pair}"] + 2)
                for d in range(2 * DT):
                    for m in range(2):
                        ins = nc.tensor.matmul(bank(SET[f"v{pair}"], d * SEQ, SEQ), v_mem[:, m, d * P:(d + 1) * P],
                                               pT[:, 2 * pair + d // DT, m, :], start=(m == 0), stop=(m == 1))
                    if d % 2 == 1:
                        ins.then_inc(pv_done, 1)

            turned_group("q0", memT_hi, memT_lo, TAKEN["memB"] + 4, "k0", KD)
            turned_group("k0", xT_hi, xT_lo, TAKEN["q0"] + 4, "q1", 6)
            scores(0)
            group("q1", xT_hi, xT_lo, 6, 10)
            turn_probs(0)
            group("q1", xT_hi, xT_lo, 10, KD)
            turned_group("q1", memT_hi, memT_lo, TAKEN["p0"] + 2, "k1", KD)
            turned_group("k1", memT_hi, memT_lo, TAKEN["q1"] + 4, "v0", 6)
            scores(1)
            group("v0", memT_hi, memT_lo, 6, 10)
            turn_probs(1)
            group("v0", memT_hi, memT_lo, 10, KD)
            pe.wait_ge(taken, TAKEN["p1"] + 2)
            group("v1", memT_hi, memT_lo, 0, 5)
            attend(0)
            group("v1", memT_hi, memT_lo, 5, KD)
            pe.wait_ge(taken, TAKEN["pv0"] + 4)
            group("xo0", yT_hi, yT_lo, 0, 5)
            attend(1)
            group("xo0", yT_hi, yT_lo, 5, 8)
            pe.wait_ge(taken, TAKEN["pv1"] + 4)
            group("xo0", yT_hi, yT_lo, 8, KD)
            resid("xo0", 0, "xo1", yT_hi, yT_lo, TAKEN["pv1"] + 4)
            group("xo1", yT_hi, yT_lo, 8, KD)
            resid("xo1", 1, "ffn2_in0", xT_hi, xT_lo, TAKEN["xo0"] + 4)
            pe.wait_ge(taken, TAKEN["xo1"] + 4)
            group("ffn2_in0", xT_hi, xT_lo, 8, KD)
            ffn_in(2)
            ffn_out(2)


_INS = ["x", "mem", "g_ffn1", "w_ffn1_in", "w_ffn1_out", "g_mix", "w_mix_in", "conv_w", "conv_b", "g_gm_v", "w_spatial",
        "b_spatial", "w_mix_out", "g_xattn", "g_mem", "w_xq", "w_xk", "w_xv", "w_xo", "g_ffn2", "w_ffn2_in",
        "w_ffn2_out", "g_final"]


def kernel(**inputs):
    import numpy as np
    import concourse.bacc as bacc
    from concourse.bass_utils import run_bass_kernel_spmd

    nc = bacc.Bacc("TRN2", target_bir_lowering=False, num_devices=1)
    arrays, args = {}, []
    for name in _INS:
        a = np.ascontiguousarray(inputs[name])
        arrays[f"in_{name}"] = a
        args.append(nc.dram_tensor(f"in_{name}", a.shape, mybir.dt.from_np(a.dtype), kind="ExternalInput").ap())
    shape = arrays["in_x"].shape
    args.append(nc.dram_tensor("out_0", shape, F32, kind="ExternalOutput").ap())
    build(nc, *args)
    r = run_bass_kernel_spmd(nc, [arrays], core_ids=[0])
    return r.results[0]["out_0"]
```

```python
from contextlib import ExitStack

import concourse.bass as bass
from concourse import mybir

ALU = mybir.AluOpType
ACT = mybir.ActivationFunctionType
AX_X = mybir.AxisListType.X
F32 = mybir.dt.float32
F32R = mybir.dt.float32r

P = 128
TOK = 2
SEQ = TOK * P
Q = 32
BLK = 512
GW = 2 * BLK
SETW = 4 * BLK
RAW = 4
RING = 4
EPS = 1e-6
XA_HEADS = 4


def starts(steps):
    at, n = {}, 0
    for name, k in steps:
        at[name] = n
        n += k
    return at


def build(nc, x, mem, g_ffn1, w_ffn1_in, w_ffn1_out, g_mix, w_mix_in, conv_w, conv_b, g_gm_v, w_spatial, b_spatial,
          w_mix_out, g_xattn, g_mem, w_xq, w_xk, w_xv, w_xo, g_ffn2, w_ffn2_in, w_ffn2_out, g_final, out):
    D = x.shape[2]
    KD = D // P
    FF = w_ffn1_out.shape[1]
    KF = FF // P
    FG = FF // BLK
    HEADS = w_spatial.shape[1]
    HALF = GW // P
    HD = D // XA_HEADS
    DT = HD // P
    SCALE = float(HD) ** -0.5
    assert KD % RING == 0 and KF % RING == 0 and FG % 2 == 1 and D == 2 * GW and HEADS == HALF

    groups = [(f"ffn1_in{g}", KD) for g in range(FG)] + [("ffn1_out0", KF), ("ffn1_out1", KF)]
    groups += [(n, KD) for n in ("C", "H", "B", "V", "U", "mix_out0", "mix_out1", "q0", "q1", "k0", "k1", "v0", "v1",
                                 "xo0", "xo1")]
    groups += [(f"ffn2_in{g}", KD) for g in range(FG)] + [("ffn2_out0", KF), ("ffn2_out1", KF)]
    UNIT0 = starts(groups)
    UNITS = dict(groups)
    SET = {name: i % 2 for i, (name, _) in enumerate(groups)}

    def done(group):
        return UNIT0[group] + UNITS[group]

    f1 = [(f"ffn1_in{g}", 2) for g in range(FG)]
    f2 = [(f"ffn2_in{g}", 2) for g in range(FG)]
    TURN = starts([("x0", 4), ("x1", 4)] + f1 + [("ffn1_out0", 4), ("ffn1_out1", 4), ("ws", 2), ("H", 4), ("B", 4),
                  ("U", 4), ("mix_out0", 4), ("memA", 4), ("mix_out1", 4), ("memB", 4), ("q0", 4), ("q1", 4),
                  ("k0", 4), ("p0", 2), ("k1", 4), ("p1", 2), ("xo0", 4), ("xo1", 4)] + f2)
    HI = starts([("x0", 4), ("x1", 4)] + f1 + [("ffn1_out0", 4), ("ffn1_out1", 4), ("U", 4), ("mix_out0", 4),
                ("memA", 4), ("mix_out1", 4), ("memB", 4), ("q0", 4), ("q1", 4), ("k0", 4), ("p0", 2), ("k1", 4),
                ("p1", 2), ("pv0", 4), ("pv1", 4), ("xo0", 4), ("xo1", 4)] + f2)
    TAKEN = starts([("x0", 4), ("x1", 4)] + f1 + [("ffn1_out0", 4), ("ffn1_out1", 4), ("ws", 2), ("U", 4),
                   ("mix_out0", 4), ("memA", 4), ("mix_out1", 4), ("memB", 4), ("q0", 4), ("q1", 4), ("k0", 4),
                   ("p0", 2), ("k1", 4), ("p1", 2), ("pv0", 4), ("pv1", 4), ("xo0", 4), ("xo1", 4)] + f2)
    STAGED = starts([(f"ffn1_in{g}", 2) for g in range(FG)] + [(n, 2) for n in (
        "ffn1_out0", "ffn1_out1", "H", "B", "U", "mix_out0", "mix_out1", "q0", "q1", "k0", "k1", "xo0", "xo1")]
        + [(f"ffn2_in{g}", 2) for g in range(FG)] + [("ffn2_out0", 2), ("ffn2_out1", 2)])
    SQUARED = starts([(n, 2) for n in ("x0", "x1", "ffn1_out0", "ffn1_out1", "mix_out0", "mix_out1", "mem0", "mem1",
                                       "xo0", "xo1", "ffn2_out0", "ffn2_out1")])
    NORM = starts([(n, 1) for n in ("x", "ffn1", "v", "mix", "mem", "xo", "final0", "final1")])

    BASE = (nc.sbuf_base + 31) // 32 * 32
    KB = 1024
    place = {"at": BASE}

    def put(name, shape, dt, at=None):
        size = 4
        for s in shape[1:]:
            size *= s
        if at is None:
            at = place["at"]
            place["at"] = at + (size + 31) // 32 * 32
        return nc.alloc_sbuf_tensor_at(name, shape, dt, offset=at)

    h = put("h", [P, TOK, D], F32)
    xT_hi = put("xT_hi", [P, KD, SEQ], F32R)
    xT_lo = put("xT_lo", [P, KD, SEQ], F32R)
    raw = put("raw", [P, RAW, GW], F32)
    w_hi = put("w_hi", [P, RING, GW], F32R)
    w_lo = put("w_lo", [P, RING, GW], F32R)
    stage = put("stage", [P, TOK, GW], F32)
    scratch = put("scratch", [P, GW], F32)
    ident = put("ident", [P, P], F32)
    rows = put("rows", [P, P], F32)
    cols = put("cols", [P, P], F32)
    ssq = put("ssq", [P, 2, TOK], F32)
    rstd = put("rstd", [P, TOK], F32)
    rstd_mem = put("rstd_mem", [P, TOK], F32)
    rstd_v = put("rstd_v", [P, TOK * HEADS], F32)
    ssv = put("ssv", [P, TOK * HEADS], F32)
    small = put("small", [P, 4, TOK * HEADS], F32)
    smax = put("smax", [P, 4], F32)
    nbias = put("nbias", [P, 4], F32)
    rsum = put("rsum", [P, 4], F32)
    rinv = put("rinv", [P, 4], F32)
    extra = place["at"]
    g_v = put("g_v", [P, GW], F32, at=extra)
    ws = put("ws", [P, HEADS, P], F32, at=extra + 4 * KB)
    pT_hi = put("pT_hi", [P, XA_HEADS * 2, SEQ], F32R, at=extra)
    g_fin = put("g_fin", [P, D], F32, at=extra)
    big = extra + 8 * KB
    hidT_hi = put("hidT_hi", [P, KF, SEQ], F32R, at=big)
    hidT_lo = put("hidT_lo", [P, KF, SEQ], F32R, at=big + KF * KB)
    yT_hi = put("yT_hi", [P, KD, SEQ], F32R, at=big)
    yT_lo = put("yT_lo", [P, KD, SEQ], F32R, at=big + 16 * KB)
    memT_hi = put("memT_hi", [P, KD, SEQ], F32R, at=big + 32 * KB)
    memT_lo = put("memT_lo", [P, KD, SEQ], F32R, at=big + 48 * KB)
    c_buf = put("c_buf", [P, TOK, GW], F32, at=big + 32 * KB)
    zT = put("zT", [P, HALF, SEQ], F32, at=big + 40 * KB)
    convT = put("convT", [P, HALF, SEQ], F32, at=big + 48 * KB)
    v_buf = put("v_buf", [P, TOK, GW], F32, at=big + 56 * KB)
    wsT = put("wsT", [P, HEADS, P], F32, at=big + 64 * KB)
    sg = put("sg", [P, TOK, GW], F32, at=big + 80 * KB)
    mem_nat = put("mem_nat", [P, TOK, D], F32, at=big + 64 * KB)
    v_hi = put("v_hi", [P, TOK, GW], F32R, at=big + 64 * KB)
    v_lo = put("v_lo", [P, TOK, GW], F32R, at=big + 72 * KB)
    pT_lo = put("pT_lo", [P, XA_HEADS * 2, SEQ], F32R, at=big + 80 * KB)
    qT_hi, qT_lo = yT_hi, yT_lo
    kT_hi, kT_lo = xT_hi, xT_lo
    assert big + 2 * KF * KB <= nc.sbuf_usable_end

    vectors = [("g_ffn1", g_ffn1[0], KD), ("g_mix", g_mix[0], KD), ("g_xattn", g_xattn[0], KD), ("g_mem", g_mem[0], KD),
               ("g_ffn2", g_ffn2[0], KD), ("conv_w", conv_w[0].rearrange("k c -> (k c)"), 3 * HALF),
               ("conv_b", conv_b[0], HALF), ("b_spatial", b_spatial[0].rearrange("h t -> (h t)"), HEADS)]
    ROW = starts([(n, k) for n, _, k in vectors])
    NROWS = sum(k for _, _, k in vectors)

    def col(name, k):
        return cols[:, ROW[name] + k:ROW[name] + k + 1]

    with ExitStack() as ctx:
        def sem(name):
            return ctx.enter_context(nc.semaphore(name))

        ps = ctx.enter_context(nc.psum_tensor("ps", [P, 2 * SETW], F32))

        def bank(s, c0, n):
            return ps[:, s * SETW + c0:s * SETW + c0 + n]

        raw_loaded = [sem(f"raw_loaded{i}") for i in range(RAW)]
        hi_ready = sem("hi_ready")
        lo_ready = sem("lo_ready")
        unit_used = sem("unit_used")
        staged = sem("staged")
        turned = sem("turned")
        hi_taken = sem("hi_taken")
        taken = sem("taken")
        silu_ready = sem("silu_ready")
        squared = sem("squared")
        ms_ready = sem("ms_ready")
        root_ready = sem("root_ready")
        rstd_ready = sem("rstd_ready")
        dve_step = sem("dve_step")
        act_step = sem("act_step")
        x_loaded = [sem(f"x_loaded{i}") for i in range(D // BLK)]
        gain_loaded = sem("gain_loaded")
        rows_loaded = sem("rows_loaded")
        gv_loaded = sem("gv_loaded")
        ws_loaded = sem("ws_loaded")
        mem_loaded = sem("mem_loaded")
        gfin_loaded = sem("gfin_loaded")
        ident_zero = sem("ident_zero")
        ident_ready = sem("ident_ready")
        ws_masked = sem("ws_masked")
        rows_turned = sem("rows_turned")
        cols_ready = sem("cols_ready")
        c_taken = sem("c_taken")
        z_taken = sem("z_taken")
        conv_done = sem("conv_done")
        yc_product = sem("yc_product")
        yc_hi = sem("yc_hi")
        yc_ready = sem("yc_ready")
        v_squared = sem("v_squared")
        vn_ready = sem("vn_ready")
        gated = sem("gated")
        sg_ready = sem("sg_ready")
        scored = sem("scored")
        nbias_ready = sem("nbias_ready")
        exp_ready = sem("exp_ready")
        probs_ready = sem("probs_ready")
        v_rounded = sem("v_rounded")
        v_split = sem("v_split")
        pv_done = sem("pv_done")
        last_tile = sem("last_tile")
        gained = sem("gained")
        out_ready = [sem(f"out_ready{c}") for c in range(2)]
        out_stored = sem("out_stored")

        block = ctx.enter_context(nc.Block())

        def ffn_in_src(w, col0):
            v = w[0].rearrange("(k p) (s n) -> k p s n", p=P, s=2)
            return lambda k: v[k][:, :, bass.ds(col0, BLK)]

        def cols_src(w, col0):
            v = w[0].rearrange("(k p) n -> k p n", p=P)
            return lambda k: v[k][:, col0:col0 + GW]

        @block.sync
        def _(sp):
            def load_units(src, unit0, n):
                for k in range(n):
                    dst = raw[:, k % RAW, :]
                    if len(src(k).shape) == 3:
                        dst = dst.rearrange("p (s n) -> p s n", s=2)
                    if not (isinstance(unit0, int) and unit0 + k < RAW):
                        sp.wait_ge(lo_ready, unit0 + (k - RAW + 1))
                    sp.dma_start(dst, src(k)).then_inc(raw_loaded[k % RAW], 16)

            def load_ffn_in(f, w):
                u0 = UNIT0[f"ffn{f}_in0"]
                load_units(ffn_in_src(w, 0), u0, KD)
                with sp.Fori(0, FG // 2) as i:
                    for j in range(2):
                        load_units(ffn_in_src(w, i * GW + (1 + j) * BLK), i * (2 * KD) + (u0 + (1 + j) * KD), KD)

            def load_pair(name, w, n):
                for c in range(2):
                    load_units(cols_src(w, c * GW), UNIT0[f"{name}{c}"], n)

            xv = x[0].rearrange("(t p) n -> p t n", p=P)
            for c in range(D // BLK):
                sp.dma_start(h[:, :, c * BLK:(c + 1) * BLK], xv[:, :, c * BLK:(c + 1) * BLK]).then_inc(x_loaded[c], 16)
            load_ffn_in(1, w_ffn1_in)
            load_pair("ffn1_out", w_ffn1_out, KF)
            for name, c in (("C", 1), ("H", 2), ("B", 0), ("V", 4), ("U", 3)):
                load_units(cols_src(w_mix_in, c * GW), UNIT0[name], KD)
            sp.wait_ge(gated, 4)
            sp.dma_start(mem_nat[:, :, :], mem[0].rearrange("(t p) n -> p t n", p=P)).then_inc(mem_loaded, 16)
            load_pair("mix_out", w_mix_out, KD)
            load_pair("q", w_xq, KD)
            load_pair("k", w_xk, KD)
            load_pair("v", w_xv, KD)
            load_pair("xo", w_xo, KD)
            sp.wait_ge(pv_done, 8)
            sp.dma_start(g_fin[:, :], g_final.partition_broadcast(P)).then_inc(gfin_loaded, 16)
            load_ffn_in(2, w_ffn2_in)
            load_pair("ffn2_out", w_ffn2_out, KF)
            ov = out[0].rearrange("(t p) n -> p t n", p=P)
            for t in range(TOK):
                for c in range(2):
                    sp.wait_ge(out_ready[c], t + 1)
                    sp.dma_start(ov[:, t, c * GW:(c + 1) * GW], h[:, t, c * GW:(c + 1) * GW]).then_inc(out_stored, 16)
            sp.wait_ge(out_stored, 16 * TOK * 2)

        @block.gpsimd
        def _(pool):
            pool.memset(ident[:, :], 0.0).then_inc(ident_zero, 1)
            pool.wait_ge(ident_zero, 1)
            pool.affine_select(out=ident[:, :], in_=ident[:, :], compare_op=ALU.not_equal, fill=1.0, base=0,
                               pattern=[[-1, P]], channel_multiplier=1).then_inc(ident_ready, 1)
            pool.wait_ge(ws_loaded, 16)
            pool.affine_select(out=ws[:, :, :], in_=ws[:, :, :], compare_op=ALU.is_ge, fill=0.0, base=0,
                               pattern=[[0, HEADS], [-1, P]], channel_multiplier=1).then_inc(ws_masked, 1)

        @block.scalar
        def _(act):
            def hi_units(unit0, k0, k1):
                for k in range(k0, k1):
                    act.wait_ge(raw_loaded[k % RAW], unit0 * (16 // RAW) + 16 * (k // RAW + 1))
                    if not (isinstance(unit0, int) and unit0 + k < RING):
                        act.wait_ge(unit_used, unit0 + (k - RING + 1))
                    nc.scalar.activation(w_hi[:, k % RING, :], raw[:, k % RAW, :], ACT.Copy).then_inc(hi_ready, 1)

            def hi_scaled(dst, k0, g, s, name, b0=0, b1=4):
                for b in range(b0, b1):
                    act.wait_ge(turned, TURN[name] + b + 1)
                    for j in range(2):
                        k = 2 * b + j
                        ins = nc.scalar.activation(dst[:, k0 + k, :], bank(s, k * SEQ, SEQ), ACT.Copy, scale=col(g, k0 + k))
                    ins.then_inc(hi_taken, 1)

            def hi_plain(dst, k0, s, banks, ready, first, b0=0):
                for b in range(banks):
                    act.wait_ge(ready, first + b + 1)
                    nc.scalar.activation(dst[:, bass.ds(k0 + 2 * b, 2), :].rearrange("p k t -> p (k t)"),
                                         bank(s, (b0 + b) * BLK, BLK), ACT.Copy).then_inc(hi_taken, 1)

            def squares(src, c, name):
                for t in range(TOK):
                    if SQUARED[name] + t > 0:
                        act.wait_ge(squared, SQUARED[name] + t)
                    nc.scalar.activation(scratch[:, :], src[:, t, c * GW:(c + 1) * GW], ACT.Square,
                                         accum_out=ssq[:, c, t:t + 1]).then_inc(squared, 1)

            def root(norm, n):
                act.wait_ge(ms_ready, NORM[norm] + 1)
                nc.scalar.activation(small[:, 1, 0:n], small[:, 0, 0:n], ACT.Sqrt).then_inc(root_ready, 1)

            def silu(s, used):
                act.wait_ge(unit_used, used)
                for t in range(TOK):
                    nc.scalar.activation(scratch[:, t * BLK:(t + 1) * BLK], bank(s, t * GW, BLK), ACT.Silu,
                                         scale=rstd[:, t:t + 1]).then_inc(silu_ready, 1)

            def resid(name, c, dst, g, first, half):
                hi_units(first, 0, 4)
                act.wait_ge(staged, STAGED[name] + TOK)
                squares(h, c, name)
                hi_units(first, 4, 8)
                hi_scaled(dst, c * HALF, g, half, name)

            def ffn_in(f, norm):
                u0 = UNIT0[f"ffn{f}_in0"]
                act.wait_ge(rstd_ready, NORM[norm] + 1)
                with act.Fori(0, FG // 2) as i:
                    for j in range(2):
                        unit0 = i * (2 * KD) + (u0 + (1 + j) * KD)
                        hi_units(unit0, 0, 4)
                        silu(j, unit0)
                        hi_units(unit0, 4, 11)
                        hi_plain(hidT_hi, i * 8 + 4 * j, j, 2, turned, i * 4 + (TURN[f"ffn{f}_in0"] + 2 * j))
                        hi_units(unit0, 11, KD)

            def ffn_out(f):
                last = f"ffn{f}_in{FG - 1}"
                u0 = UNIT0[f"ffn{f}_out0"]
                hi_units(u0, 0, 4)
                silu(SET[last], u0)
                hi_units(u0, 4, 11)
                hi_plain(hidT_hi, 4 * (FG - 1), SET[last], 2, turned, TURN[last])
                hi_units(u0, 11, KF)

            def load_rows(name, v, k, landed):
                act.dma_start(rows[ROW[name]:ROW[name] + k, :], v.rearrange("(r c) -> r c", c=P)).then_inc(landed, 16)

            load_rows(*vectors[0], gain_loaded)
            act.wait_ge(cols_ready, 1)
            for b in range(4):
                hi_scaled(xT_hi, 0, "g_ffn1", 1, "x0", b, b + 1)
                hi_units(0, b, b + 1)
            for v in vectors[1:]:
                load_rows(*v, rows_loaded)
            act.dma_start(ws[:, :, :], w_spatial[0].rearrange("h t s -> t h s")).then_inc(ws_loaded, 16)
            act.dma_start(g_v[:, :], g_gm_v[0].partition_broadcast(P)).then_inc(gv_loaded, 16)
            for c in range(2):
                act.wait_ge(x_loaded[2 * c], 16)
                act.wait_ge(x_loaded[2 * c + 1], 16)
                squares(h, c, f"x{c}")
            hi_units(0, 4, 7)
            hi_scaled(xT_hi, HALF, "g_ffn1", 1, "x1")
            hi_units(0, 7, 8)
            root("x", TOK)
            hi_units(0, 8, KD)
            ffn_in(1, "x")
            ffn_out(1)
            u = UNIT0["ffn1_out1"]
            resid("ffn1_out0", 0, xT_hi, "g_mix", u, SET["ffn1_out0"])
            hi_units(u, 8, KF)
            u = UNIT0["C"]
            resid("ffn1_out1", 1, xT_hi, "g_mix", u, SET["ffn1_out1"])
            root("ffn1", TOK)
            hi_units(u, 8, KD)
            u = UNIT0["H"]
            hi_units(u, 0, 4)
            act.wait_ge(unit_used, done("C"))
            act.wait_ge(rstd_ready, NORM["ffn1"] + 1)
            for t in range(TOK):
                nc.scalar.activation(c_buf[:, t, :], bank(SET["C"], t * GW, GW), ACT.Copy,
                                     scale=rstd[:, t:t + 1]).then_inc(c_taken, 1)
            hi_units(u, 4, KD)
            u = UNIT0["B"]
            hi_units(u, 0, 8)
            for b in range(4):
                act.wait_ge(turned, TURN["H"] + b + 1)
                nc.scalar.activation(zT[:, 2 * b:2 * b + 2, :].rearrange("p k t -> p (k t)"), bank(SET["H"], b * BLK, BLK),
                                     ACT.Copy)
                for k in (2 * b, 2 * b + 1):
                    nc.scalar.activation(convT[:, k, :], bank(SET["H"], k * SEQ, SEQ), ACT.Identity,
                                         scale=col("conv_w", 2 * HALF + k), bias=col("conv_b", k)).then_inc(z_taken, 1)
            hi_units(u, 8, KD)
            u = UNIT0["V"]
            hi_units(u, 0, 9)
            act.wait_ge(yc_product, 1)
            nc.scalar.activation(yT_hi[:, 0:HALF, :], convT[:, :, :], ACT.Copy).then_inc(yc_hi, 1)
            hi_units(u, 9, KD)
            u = UNIT0["U"]
            hi_units(u, 0, 4)
            act.wait_ge(unit_used, done("V"))
            for t in range(TOK):
                nc.scalar.activation(v_buf[:, t, :], bank(SET["V"], t * GW, GW), ACT.Copy,
                                     scale=rstd[:, t:t + 1]).then_inc(act_step, 1)
            act.wait_ge(act_step, TOK)
            act.wait_ge(staged, STAGED["H"] + TOK)
            nc.scalar.activation(c_buf[:, :, :], v_buf[:, :, :], ACT.Square).then_inc(v_squared, 1)
            hi_units(u, 4, 7)
            root("v", TOK * HEADS)
            hi_units(u, 7, 14)
            for hd in range(HEADS):
                if hd % 2 == 0:
                    act.wait_ge(gated, hd // 2 + 1)
                nc.scalar.activation(sg[:, :, hd * P:(hd + 1) * P],
                                     bank(SET["V"], hd * SEQ, SEQ).rearrange("p (t c) -> p t c", t=TOK), ACT.Identity,
                                     bias=col("b_spatial", hd)).then_inc(sg_ready, 1)
            hi_units(u, 14, KD)
            u = UNIT0["mix_out0"]
            hi_units(u, 0, 8)
            hi_plain(yT_hi, HALF, SET["U"], 4, turned, TURN["U"])
            hi_units(u, 8, KD)
            u = UNIT0["mix_out1"]
            resid("mix_out0", 0, xT_hi, "g_xattn", u, SET["mix_out0"])
            hi_units(u, 8, 13)
            hi_scaled(memT_hi, 0, "g_mem", SET["mix_out0"], "memA")
            hi_units(u, 13, KD)
            u = UNIT0["q0"]
            resid("mix_out1", 1, xT_hi, "g_xattn", u, SET["mix_out1"])
            root("mix", TOK)
            hi_units(u, 8, 13)
            hi_scaled(memT_hi, HALF, "g_mem", SET["mix_out1"], "memB")
            hi_units(u, 13, KD)
            u = UNIT0["q1"]
            hi_units(u, 0, 4)
            for c in range(2):
                squares(mem_nat, c, f"mem{c}")
            hi_units(u, 4, 8)
            hi_plain(qT_hi, 0, SET["q0"], 4, turned, TURN["q0"])
            root("mem", TOK)
            hi_units(u, 8, KD)
            u = UNIT0["k0"]
            hi_units(u, 0, 8)
            hi_plain(qT_hi, HALF, SET["q1"], 4, turned, TURN["q1"])
            hi_units(u, 8, KD)
            for pair, running in enumerate(("k1", "v0")):
                u = UNIT0[running]
                s = SET[f"k{pair}"]
                hi_units(u, 0, 8)
                hi_plain(kT_hi, pair * HALF, s, 4, turned, TURN[f"k{pair}"])
                hi_units(u, 8, 11)
                act.wait_ge(nbias_ready, pair + 1)
                for j in range(4):
                    nc.scalar.activation(scratch[:, j * SEQ:(j + 1) * SEQ], bank(s, j * SEQ, SEQ), ACT.Exp,
                                         bias=nbias[:, j:j + 1], scale=SCALE, accum_out=rsum[:, j:j + 1]
                                         ).then_inc(exp_ready, 1)
                hi_units(u, 11, 15)
                hi_plain(pT_hi, 4 * pair, s, 2, turned, TURN[f"p{pair}"], b0=2)
                hi_units(u, 15, KD)
            for pair, running in enumerate(("v1", "xo0")):
                u = UNIT0[running]
                s = SET[f"v{pair}"]
                hi_units(u, 0, 4)
                act.wait_ge(unit_used, done(f"v{pair}"))
                act.wait_ge(rstd_ready, NORM["mem"] + 1)
                for t in range(TOK):
                    nc.scalar.activation(v_hi[:, t, :], bank(s, t * GW, GW), ACT.Copy,
                                         scale=rstd_mem[:, t:t + 1]).then_inc(v_rounded, 1)
                hi_units(u, 4, 9)
                hi_plain(yT_hi, pair * HALF, s, 4, pv_done, 4 * pair)
                hi_units(u, 9, KD)
            u = UNIT0["xo1"]
            resid("xo0", 0, xT_hi, "g_ffn2", u, SET["xo0"])
            hi_units(u, 8, KD)
            u = UNIT0["ffn2_in0"]
            resid("xo1", 1, xT_hi, "g_ffn2", u, SET["xo1"])
            root("xo", TOK)
            hi_units(u, 8, KD)
            ffn_in(2, "xo")
            ffn_out(2)
            u = UNIT0["ffn2_out1"]
            hi_units(u, 0, 4)
            act.wait_ge(staged, STAGED["ffn2_out0"] + TOK)
            squares(h, 0, "ffn2_out0")
            hi_units(u, 4, KF)
            for t in range(TOK):
                act.wait_ge(staged, STAGED["ffn2_out1"] + t + 1)
                act.wait_ge(squared, SQUARED["ffn2_out1"] + t)
                nc.scalar.activation(scratch[:, :], h[:, t, GW:D], ACT.Square, accum_out=ssq[:, 1, t:t + 1]).then_inc(squared, 1)
                root(f"final{t}", 1)
                act.wait_ge(gained, TOK + t + 1)
                act.wait_ge(rstd_ready, NORM[f"final{t}"] + 1)
                nc.scalar.activation(h[:, t, GW:D], stage[:, t, :], ACT.Copy, scale=rstd[:, t:t + 1]).then_inc(out_ready[1], 1)

        @block.vector
        def _(dve):
            steps = [0]

            def chain(ins):
                ins.then_inc(dve_step, 1)
                steps[0] += 1
                dve.wait_ge(dve_step, steps[0])

            def lo_units(unit0, k0, k1):
                for k in range(k0, k1):
                    dve.wait_ge(hi_ready, unit0 + (k + 1))
                    nc.vector.tensor_tensor(w_lo[:, k % RING, :], raw[:, k % RAW, :], w_hi[:, k % RING, :].bitcast(F32),
                                            ALU.subtract).then_inc(lo_ready, 1)

            def lo_scaled(dst, hi, k0, g, s, name, b0=0, b1=4):
                for b in range(b0, b1):
                    dve.wait_ge(hi_taken, HI[name] + b + 1)
                    for j in range(2):
                        k = 2 * b + j
                        ins = nc.vector.scalar_tensor_tensor(out=dst[:, k0 + k, :], in0=bank(s, k * SEQ, SEQ),
                                                             scalar=col(g, k0 + k), in1=hi[:, k0 + k, :].bitcast(F32),
                                                             op0=ALU.mult, op1=ALU.subtract)
                    ins.then_inc(taken, 1)

            def lo_plain(dst, hi, k0, s, banks, first, b0=0):
                for b in range(banks):
                    dve.wait_ge(hi_taken, first + b + 1)
                    nc.vector.tensor_tensor(dst[:, bass.ds(k0 + 2 * b, 2), :].rearrange("p k t -> p (k t)"),
                                            bank(s, (b0 + b) * BLK, BLK),
                                            hi[:, bass.ds(k0 + 2 * b, 2), :].rearrange("p k t -> p (k t)").bitcast(F32),
                                            ALU.subtract).then_inc(taken, 1)

            def norm(name, total, count, res):
                ms, rt, inv, t = (small[:, i, 0:res.shape[1]] for i in range(4))
                if isinstance(total, tuple):
                    chain(nc.vector.tensor_tensor(t, total[0], total[1], ALU.add))
                    total = t
                nc.vector.tensor_scalar(ms, total, 1.0 / count, EPS, ALU.mult, ALU.add).then_inc(ms_ready, 1)
                dve.wait_ge(root_ready, NORM[name] + 1)
                chain(nc.vector.reciprocal(inv, rt))
                chain(nc.vector.tensor_tensor(t, inv, inv, ALU.mult))
                chain(nc.vector.tensor_tensor(t, t, ms, ALU.mult))
                chain(nc.vector.tensor_scalar(t, t, -0.5, 1.5, ALU.mult, ALU.add))
                nc.vector.tensor_tensor(res, inv, t, ALU.mult).then_inc(rstd_ready, 1)
                dve.wait_ge(rstd_ready, NORM[name] + 1)

            def add_resid(name, c, coef):
                dve.wait_ge(unit_used, done(name))
                for t in range(TOK):
                    hs = h[:, t, c * GW:(c + 1) * GW]
                    nc.vector.scalar_tensor_tensor(out=hs, in0=bank(SET[name], t * GW, GW), scalar=coef, in1=hs,
                                                   op0=ALU.mult, op1=ALU.add).then_inc(staged, 1)

            def resid(name, c, coef, g, first):
                lo_units(first, 0, 4)
                add_resid(name, c, coef)
                lo_units(first, 4, 8)
                lo_scaled(xT_lo, xT_hi, c * HALF, g, SET[name], name)

            def turn_quadrant(q, s, tiles):
                for j in range(P // Q):
                    dst = bank(s, 0, tiles * SEQ).rearrange("p (k t b) -> p t k b", t=TOK, b=P)
                    src = stage[:, :, 0:tiles * P].rearrange("p t (k c) -> p t k c", c=P)
                    ins = nc.vector.transpose(dst[j * Q:(j + 1) * Q, :, :, q * Q:(q + 1) * Q],
                                              src[q * Q:(q + 1) * Q, :, :, j * Q:(j + 1) * Q])
                if q == P // Q - 1:
                    ins.then_inc(turned, tiles // 2)

            def gate(s, silus):
                for t in range(TOK):
                    dve.wait_ge(silu_ready, silus + t + 1)
                    nc.vector.scalar_tensor_tensor(out=stage[:, t, 0:BLK], in0=bank(s, t * GW + BLK, BLK),
                                                   scalar=rstd[:, t:t + 1], in1=scratch[:, t * BLK:(t + 1) * BLK],
                                                   op0=ALU.mult, op1=ALU.mult).then_inc(staged, 1)

            def ffn_in(f):
                u0 = UNIT0[f"ffn{f}_in0"]
                s0 = (f - 1) * 2 * FG
                with dve.Fori(0, FG // 2) as i:
                    for j in range(2):
                        unit0 = i * (2 * KD) + (u0 + (1 + j) * KD)
                        lo_units(unit0, 0, 4)
                        gate(j, i * 4 + (s0 + 2 * j))
                        lo_units(unit0, 4, 5)
                        dve.wait_ge(staged, i * 4 + (STAGED[f"ffn{f}_in0"] + 2 * j + TOK))
                        for q in range(P // Q):
                            turn_quadrant(q, j, BLK // P)
                            lo_units(unit0, 5 + q, 6 + q)
                        lo_units(unit0, 9, 11)
                        lo_plain(hidT_lo, hidT_hi, i * 8 + 4 * j, j, 2, i * 4 + (HI[f"ffn{f}_in0"] + 2 * j))
                        lo_units(unit0, 11, KD)

            def ffn_out(f):
                last = f"ffn{f}_in{FG - 1}"
                u0 = UNIT0[f"ffn{f}_out0"]
                lo_units(u0, 0, 4)
                gate(SET[last], (f - 1) * 2 * FG + 2 * (FG - 1))
                lo_units(u0, 4, 5)
                dve.wait_ge(staged, STAGED[last] + TOK)
                for q in range(P // Q):
                    turn_quadrant(q, SET[last], BLK // P)
                    lo_units(u0, 5 + q, 6 + q)
                lo_units(u0, 9, 11)
                lo_plain(hidT_lo, hidT_hi, 4 * (FG - 1), SET[last], 2, HI[last])
                lo_units(u0, 11, KF)

            def scaled(name, scale):
                dve.wait_ge(unit_used, done(name))
                for t in range(TOK):
                    nc.vector.tensor_scalar(stage[:, t, :], bank(SET[name], t * GW, GW), scale[:, t:t + 1], None,
                                            ALU.mult).then_inc(staged, 1)

            halves = (ssq[:, 0, :], ssq[:, 1, :])
            dve.wait_ge(rows_turned, 1)
            nc.vector.tensor_copy(cols[:, 0:KD], bank(0, 0, KD)).then_inc(cols_ready, 1)
            dve.wait_ge(cols_ready, 1)
            for b in range(4):
                lo_scaled(xT_lo, xT_hi, 0, "g_ffn1", 1, "x0", b, b + 1)
                lo_units(0, b, b + 1)
            lo_units(0, 4, 7)
            lo_scaled(xT_lo, xT_hi, HALF, "g_ffn1", 1, "x1")
            lo_units(0, 7, 8)
            dve.wait_ge(squared, SQUARED["x1"] + 2)
            norm("x", halves, D, rstd[:, :])
            lo_units(0, 8, 13)
            dve.wait_ge(rows_turned, 2)
            nc.vector.tensor_copy(cols[:, KD:NROWS], bank(1, KD, NROWS - KD)).then_inc(cols_ready, 1)
            dve.wait_ge(cols_ready, 2)
            lo_units(0, 13, KD)
            ffn_in(1)
            ffn_out(1)
            u = UNIT0["ffn1_out1"]
            resid("ffn1_out0", 0, 0.5, "g_mix", u)
            lo_units(u, 8, KF)
            u = UNIT0["C"]
            resid("ffn1_out1", 1, 0.5, "g_mix", u)
            dve.wait_ge(squared, SQUARED["ffn1_out1"] + 2)
            norm("ffn1", halves, D, rstd[:, :])
            lo_units(u, 8, 13)
            for b in range(2):
                dve.wait_ge(turned, TURN["ws"] + b + 1)
                nc.vector.tensor_copy(wsT[:, 4 * b:4 * b + 4, :].rearrange("s h t -> s (h t)"),
                                      bank(SET["ffn1_out1"], b * BLK, BLK)).then_inc(taken, 1)
            lo_units(u, 13, KD)
            lo_units(UNIT0["H"], 0, KD)
            u = UNIT0["B"]
            lo_units(u, 0, 4)
            dve.wait_ge(unit_used, done("H"))
            for t in range(TOK):
                dve.wait_ge(c_taken, t + 1)
                nc.vector.scalar_tensor_tensor(out=stage[:, t, :], in0=bank(SET["H"], t * GW, GW), scalar=rstd[:, t:t + 1],
                                               in1=c_buf[:, t, :], op0=ALU.mult, op1=ALU.mult).then_inc(staged, 1)
            lo_units(u, 4, 12)
            dve.wait_ge(z_taken, HALF)
            for shift in (1, 2):
                for k in range(HALF):
                    y = convT[:, k, shift:SEQ]
                    ins = nc.vector.scalar_tensor_tensor(out=y, in0=zT[:, k, 0:SEQ - shift],
                                                         scalar=col("conv_w", (2 - shift) * HALF + k), in1=y,
                                                         op0=ALU.mult, op1=ALU.add)
                    ins.then_inc(conv_done, 1)
                dve.wait_ge(conv_done, HALF * shift)
            lo_units(u, 12, KD)
            u = UNIT0["V"]
            lo_units(u, 0, 4)
            scaled("B", rstd)
            lo_units(u, 4, 8)
            cv = convT[:, :, :].rearrange("p k t -> p (k t)")
            dve.wait_ge(turned, TURN["B"] + 4)
            nc.vector.tensor_tensor(cv, cv, bank(SET["B"], 0, SETW), ALU.mult).then_inc(yc_product, 1)
            lo_units(u, 8, 10)
            dve.wait_ge(yc_product, 1)
            dve.wait_ge(yc_hi, 1)
            nc.vector.tensor_tensor(yT_lo[:, 0:HALF, :], convT[:, :, :], yT_hi[:, 0:HALF, :].bitcast(F32),
                                    ALU.subtract).then_inc(yc_ready, 1)
            lo_units(u, 10, KD)
            u = UNIT0["U"]
            lo_units(u, 0, 6)
            dve.wait_ge(v_squared, 1)
            chain(nc.vector.tensor_reduce(ssv[:, :], c_buf[:, :, :].rearrange("p t (h c) -> p (t h) c", c=P), AX_X, ALU.add))
            norm("v", ssv[:, :], P, rstd_v[:, :])
            vv = v_buf[:, :, :].rearrange("p t (h c) -> p (t h) c", c=P)
            chain(nc.vector.tensor_tensor(vv, vv, rstd_v[:, :].unsqueeze(2).to_broadcast([P, TOK * HEADS, P]), ALU.mult))
            lo_units(u, 6, 8)
            dve.wait_ge(gv_loaded, 16)
            for t in range(TOK):
                nc.vector.tensor_tensor(v_buf[:, t, :], v_buf[:, t, :], g_v[:, :], ALU.mult).then_inc(vn_ready, 1)
            lo_units(u, 8, KD)
            u = UNIT0["mix_out0"]
            lo_units(u, 0, 4)
            dve.wait_ge(unit_used, done("U"))
            dve.wait_ge(sg_ready, HEADS)
            for t in range(TOK):
                nc.vector.scalar_tensor_tensor(out=stage[:, t, :], in0=bank(SET["U"], t * GW, GW), scalar=rstd[:, t:t + 1],
                                               in1=sg[:, t, :], op0=ALU.mult, op1=ALU.mult).then_inc(staged, 1)
            lo_units(u, 4, 8)
            lo_plain(yT_lo, yT_hi, HALF, SET["U"], 4, HI["U"])
            lo_units(u, 8, KD)
            u = UNIT0["mix_out1"]
            resid("mix_out0", 0, 1.0, "g_xattn", u)
            lo_units(u, 8, 13)
            lo_scaled(memT_lo, memT_hi, 0, "g_mem", SET["mix_out0"], "memA")
            lo_units(u, 13, KD)
            u = UNIT0["q0"]
            resid("mix_out1", 1, 1.0, "g_xattn", u)
            dve.wait_ge(squared, SQUARED["mix_out1"] + 2)
            norm("mix", halves, D, rstd[:, :])
            lo_units(u, 8, 13)
            lo_scaled(memT_lo, memT_hi, HALF, "g_mem", SET["mix_out1"], "memB")
            lo_units(u, 13, KD)

            def turned_qk(name, scale, dst, hi, k0, u):
                lo_units(u, 0, 4)
                scaled(name, scale)
                lo_units(u, 4, 8)
                lo_plain(dst, hi, k0, SET[name], 4, HI[name])

            u = UNIT0["q1"]
            turned_qk("q0", rstd, qT_lo, qT_hi, 0, u)
            dve.wait_ge(squared, SQUARED["mem1"] + 2)
            norm("mem", halves, D, rstd_mem[:, :])
            lo_units(u, 8, KD)
            u = UNIT0["k0"]
            turned_qk("q1", rstd, qT_lo, qT_hi, HALF, u)
            lo_units(u, 8, KD)
            for pair, running in enumerate(("k1", "v0")):
                u = UNIT0[running]
                name = f"k{pair}"
                turned_qk(name, rstd_mem, kT_lo, kT_hi, pair * HALF, u)
                lo_units(u, 8, 11)
                dve.wait_ge(scored, pair + 1)
                chain(nc.vector.tensor_reduce(smax[:, :], bank(SET[name], 0, GW).rearrange("p (j m) -> p j m", j=4),
                                              AX_X, ALU.max))
                nc.vector.tensor_scalar(nbias[:, :], smax[:, :], -SCALE, None, ALU.mult).then_inc(nbias_ready, 1)
                dve.wait_ge(exp_ready, 4 * (pair + 1))
                chain(nc.vector.reciprocal(rinv[:, :], rsum[:, :]))
                pv = scratch[:, :].rearrange("p (j m) -> p j m", j=4)
                nc.vector.tensor_tensor(pv, pv, rinv[:, :].unsqueeze(2).to_broadcast([P, 4, SEQ]),
                                        ALU.mult).then_inc(probs_ready, 1)
                lo_units(u, 11, 15)
                lo_plain(pT_lo, pT_hi, 4 * pair, SET[name], 2, HI[f"p{pair}"], b0=2)
                lo_units(u, 15, KD)
            for pair, running in enumerate(("v1", "xo0")):
                u = UNIT0[running]
                s = SET[f"v{pair}"]
                lo_units(u, 0, 4)
                for t in range(TOK):
                    dve.wait_ge(v_rounded, TOK * pair + t + 1)
                    nc.vector.scalar_tensor_tensor(out=v_lo[:, t, :], in0=bank(s, t * GW, GW), scalar=rstd_mem[:, t:t + 1],
                                                   in1=v_hi[:, t, :].bitcast(F32), op0=ALU.mult,
                                                   op1=ALU.subtract).then_inc(v_split, 1)
                lo_units(u, 4, 9)
                lo_plain(yT_lo, yT_hi, pair * HALF, s, 4, HI[f"pv{pair}"])
                lo_units(u, 9, KD)
            u = UNIT0["xo1"]
            resid("xo0", 0, 1.0, "g_ffn2", u)
            lo_units(u, 8, KD)
            u = UNIT0["ffn2_in0"]
            resid("xo1", 1, 1.0, "g_ffn2", u)
            dve.wait_ge(squared, SQUARED["xo1"] + 2)
            norm("xo", halves, D, rstd[:, :])
            lo_units(u, 8, KD)
            ffn_in(2)
            ffn_out(2)
            u = UNIT0["ffn2_out1"]
            lo_units(u, 0, 4)
            add_resid("ffn2_out0", 0, 0.5)
            lo_units(u, 4, 8)
            dve.wait_ge(gfin_loaded, 16)
            dve.wait_ge(squared, SQUARED["ffn2_out0"] + TOK)
            for t in range(TOK):
                nc.vector.tensor_tensor(h[:, t, 0:GW], h[:, t, 0:GW], g_fin[:, 0:GW], ALU.mult).then_inc(gained, 1)
            lo_units(u, 8, KF)
            for t in range(TOK):
                if t == 0:
                    dve.wait_ge(last_tile, 1)
                else:
                    dve.wait_ge(unit_used, done("ffn2_out1"))
                nc.vector.scalar_tensor_tensor(out=h[:, t, GW:D], in0=bank(SET["ffn2_out1"], t * GW, GW), scalar=0.5,
                                               in1=h[:, t, GW:D], op0=ALU.mult, op1=ALU.add).then_inc(staged, 1)
                dve.wait_ge(staged, STAGED["ffn2_out1"] + t + 1)
                nc.vector.tensor_tensor(stage[:, t, :], h[:, t, GW:D], g_fin[:, GW:D], ALU.mult).then_inc(gained, 1)
                dve.wait_ge(squared, SQUARED["ffn2_out1"] + t + 1)
                norm(f"final{t}", (ssq[:, 0, t:t + 1], ssq[:, 1, t:t + 1]), D, rstd[:, t:t + 1])
                nc.vector.tensor_scalar(h[:, t, 0:GW], h[:, t, 0:GW], rstd[:, t:t + 1], None,
                                        ALU.mult).then_inc(out_ready[0], 1)

        @block.tensor
        def _(pe):
            def mul_units(unit0, n, k0, k1, T_hi, T_lo, s, tiles=tuple(range(TOK))):
                for k in range(k0, k1):
                    pe.wait_ge(lo_ready, unit0 + (k + 1))
                    for t in tiles:
                        for xs, ws_ in ((T_hi, w_hi), (T_hi, w_lo), (T_lo, w_hi)):
                            for b in range(2):
                                ins = nc.tensor.matmul(bank(s, t * GW + b * BLK, BLK), xs[:, k, t * P:(t + 1) * P],
                                                       ws_[:, k % RING, b * BLK:(b + 1) * BLK],
                                                       start=(k == 0 and xs is T_hi and ws_ is w_hi),
                                                       stop=(k == n - 1 and xs is T_lo))
                    if TOK - 1 in tiles:
                        ins.then_inc(unit_used, 1)
                    elif k == n - 1:
                        ins.then_inc(last_tile, 1)

            def turn(src, s, k1, k0=0):
                for k in range(k0, k1):
                    for t in range(TOK):
                        ins = nc.tensor.transpose(bank(s, k * SEQ + t * P, P), src(k, t), ident[:, :])
                    if k % 2 == 1:
                        ins.then_inc(turned, 1)

            def from_stage(k, t):
                return stage[:, t, k * P:(k + 1) * P]

            def from_half(a, c):
                return lambda k, t: a[:, t, c * GW + k * P:c * GW + (k + 1) * P]

            def group(name, T_hi, T_lo, k0, k1, **tiles):
                mul_units(UNIT0[name], UNITS[name], k0, k1, T_hi, T_lo, SET[name], **tiles)

            def mul_split(out, lhs, rhs, first, last):
                for n, (a, b) in enumerate(((0, 0), (0, 1), (1, 0))):
                    ins = nc.tensor.matmul(out, lhs[a], rhs[b], start=first and n == 0, stop=last and n == 2)
                return ins

            def ffn_in(f):
                u0 = UNIT0[f"ffn{f}_in0"]
                with pe.Fori(0, FG // 2) as i:
                    for j in range(2):
                        unit0 = i * (2 * KD) + (u0 + (1 + j) * KD)
                        s = (1 + j) % 2
                        if j == 0:
                            pe.wait_ge(taken, i * 4 + TAKEN[f"ffn{f}_in0"])
                        else:
                            pe.wait_ge(taken, i * 4 + (TAKEN[f"ffn{f}_in0"] + 2))
                        mul_units(unit0, KD, 0, KD, xT_hi, xT_lo, s)

            def ffn_out(f):
                last = f"ffn{f}_in{FG - 1}"
                a, b = f"ffn{f}_out0", f"ffn{f}_out1"
                pe.wait_ge(taken, TAKEN[last])
                group(a, hidT_hi, hidT_lo, 0, KF - 4)
                pe.wait_ge(taken, TAKEN[last] + 2)
                group(a, hidT_hi, hidT_lo, KF - 4, KF)
                group(b, hidT_hi, hidT_lo, 0, 4)
                pe.wait_ge(staged, STAGED[a] + TOK)
                if f == 1:
                    turn(from_half(h, 0), SET[a], HALF)
                    group(b, hidT_hi, hidT_lo, 4, KF)
                else:
                    group(b, hidT_hi, hidT_lo, 4, KF - RING)
                    for t in range(TOK):
                        group(b, hidT_hi, hidT_lo, KF - RING, KF, tiles=(t,))

            def resid(name, c, first, T_hi, T_lo, before):
                pe.wait_ge(taken, before)
                group(first, T_hi, T_lo, 0, 4)
                pe.wait_ge(staged, STAGED[name] + TOK)
                turn(from_half(h, c), SET[name], HALF)
                group(first, T_hi, T_lo, 4, 8)

            pe.wait_ge(ident_ready, 1)
            pe.wait_ge(gain_loaded, 16)
            nc.tensor.transpose(bank(0, 0, KD), rows[0:KD, :], ident[0:KD, 0:KD]).then_inc(rows_turned, 1)
            for q in range(2):
                pe.wait_ge(x_loaded[q], 16)
                turn(from_half(h, 0), 1, 4 * q + 4, 4 * q)
            pe.wait_ge(cols_ready, 1)
            for b in range(2):
                pe.wait_ge(taken, TAKEN["x0"] + b + 1)
                group("ffn1_in0", xT_hi, xT_lo, 2 * b, 2 * b + 2)
            pe.wait_ge(taken, TAKEN["x0"] + 4)
            for q in range(2):
                pe.wait_ge(x_loaded[2 + q], 16)
                turn(from_half(h, 1), 1, 4 * q + 4, 4 * q)
            group("ffn1_in0", xT_hi, xT_lo, 4, 8)
            pe.wait_ge(taken, TAKEN["x1"] + 4)
            group("ffn1_in0", xT_hi, xT_lo, 8, 9)
            pe.wait_ge(rows_loaded, 16 * (len(vectors) - 1))
            nc.tensor.transpose(bank(1, 0, NROWS), rows[0:NROWS, :], ident[0:NROWS, 0:NROWS]).then_inc(rows_turned, 1)
            group("ffn1_in0", xT_hi, xT_lo, 9, KD)
            pe.wait_ge(cols_ready, 2)
            ffn_in(1)
            ffn_out(1)
            resid("ffn1_out1", 1, "C", xT_hi, xT_lo, TAKEN["ffn1_out0"] + 4)
            pe.wait_ge(taken, TAKEN["ffn1_out1"] + 4)
            group("C", xT_hi, xT_lo, 8, 9)
            pe.wait_ge(ws_masked, 1)
            for hd in range(HEADS):
                ins = nc.tensor.transpose(bank(SET["ffn1_out1"], hd * P, P), ws[:, hd, :], ident[:, :])
                if hd % 4 == 3:
                    ins.then_inc(turned, 1)
            group("C", xT_hi, xT_lo, 9, KD)
            pe.wait_ge(taken, TAKEN["ws"] + 2)
            group("H", xT_hi, xT_lo, 0, KD)
            pe.wait_ge(c_taken, TOK)
            group("B", xT_hi, xT_lo, 0, 4)
            pe.wait_ge(staged, STAGED["H"] + TOK)
            turn(from_stage, SET["H"], HALF)
            group("B", xT_hi, xT_lo, 4, KD)
            pe.wait_ge(z_taken, HALF)
            group("V", xT_hi, xT_lo, 0, 4)
            pe.wait_ge(staged, STAGED["B"] + TOK)
            turn(from_stage, SET["B"], HALF)
            group("V", xT_hi, xT_lo, 4, KD)
            pe.wait_ge(yc_product, 1)
            group("U", xT_hi, xT_lo, 0, 10)
            pe.wait_ge(vn_ready, TOK)
            for hd in range(HEADS):
                ins = nc.tensor.matmul(bank(SET["V"], hd * SEQ, SEQ), wsT[:, hd, :], v_buf[:, :, hd * P:(hd + 1) * P],
                                       start=True, stop=True)
                if hd % 2 == 1:
                    ins.then_inc(gated, 1)
            group("U", xT_hi, xT_lo, 10, KD)
            pe.wait_ge(sg_ready, HEADS)
            pe.wait_ge(yc_ready, 1)
            group("mix_out0", yT_hi, yT_lo, 0, 4)
            pe.wait_ge(staged, STAGED["U"] + TOK)
            turn(from_stage, SET["U"], HALF)
            group("mix_out0", yT_hi, yT_lo, 4, 8)
            pe.wait_ge(taken, TAKEN["U"] + 4)
            group("mix_out0", yT_hi, yT_lo, 8, KD)
            resid("mix_out0", 0, "mix_out1", yT_hi, yT_lo, TAKEN["U"] + 4)
            group("mix_out1", yT_hi, yT_lo, 8, 9)
            pe.wait_ge(taken, TAKEN["mix_out0"] + 4)
            pe.wait_ge(mem_loaded, 16)
            turn(from_half(mem_nat, 0), SET["mix_out0"], HALF)
            group("mix_out1", yT_hi, yT_lo, 9, KD)
            resid("mix_out1", 1, "q0", xT_hi, xT_lo, TAKEN["memA"] + 4)
            pe.wait_ge(taken, TAKEN["mix_out1"] + 4)
            group("q0", xT_hi, xT_lo, 8, 9)
            turn(from_half(mem_nat, 1), SET["mix_out1"], HALF)
            group("q0", xT_hi, xT_lo, 9, KD)

            def turned_group(name, T_hi, T_lo, before, running, k1):
                pe.wait_ge(taken, before)
                group(running, T_hi, T_lo, 0, 4)
                pe.wait_ge(staged, STAGED[name] + TOK)
                turn(from_stage, SET[name], HALF)
                group(running, T_hi, T_lo, 4, k1)

            def scores(pair):
                pe.wait_ge(taken, TAKEN[f"k{pair}"] + 4)
                for j in range(4):
                    for d in range(DT):
                        k = pair * HALF + (j // 2) * DT + d
                        tok = slice((j % 2) * P, (j % 2 + 1) * P)
                        ins = mul_split(bank(SET[f"k{pair}"], j * SEQ, SEQ), (qT_hi[:, k, tok], qT_lo[:, k, tok]),
                                        (kT_hi[:, k, :], kT_lo[:, k, :]), d == 0, d == DT - 1)
                ins.then_inc(scored, 1)

            def turn_probs(pair):
                pe.wait_ge(probs_ready, pair + 1)
                for hd in range(2):
                    for m in range(2):
                        for t in range(TOK):
                            at = (hd * 2 + t) * SEQ + m * P
                            ins = nc.tensor.transpose(bank(SET[f"k{pair}"], GW + (hd * 2 + m) * SEQ + t * P, P),
                                                      scratch[:, at:at + P], ident[:, :])
                    ins.then_inc(turned, 1)

            def attend(pair):
                pe.wait_ge(v_split, TOK * (pair + 1))
                pe.wait_ge(taken, TAKEN[f"p{pair}"] + 2)
                for d in range(2 * DT):
                    for m in range(2):
                        dc = slice(d * P, (d + 1) * P)
                        tile = 4 * pair + 2 * (d // DT) + m
                        ins = mul_split(bank(SET[f"v{pair}"], d * SEQ, SEQ), (v_hi[:, m, dc], v_lo[:, m, dc]),
                                        (pT_hi[:, tile, :], pT_lo[:, tile, :]), m == 0, m == 1)
                    if d % 2 == 1:
                        ins.then_inc(pv_done, 1)

            turned_group("q0", xT_hi, xT_lo, TAKEN["memB"] + 4, "q1", KD)
            turned_group("q1", memT_hi, memT_lo, TAKEN["q0"] + 4, "k0", KD)
            turned_group("k0", memT_hi, memT_lo, TAKEN["q1"] + 4, "k1", 7)
            for pair, running in enumerate(("k1", "v0")):
                if pair == 1:
                    turned_group("k1", memT_hi, memT_lo, TAKEN["p0"] + 2, "v0", 7)
                scores(pair)
                group(running, memT_hi, memT_lo, 7, 11)
                turn_probs(pair)
                group(running, memT_hi, memT_lo, 11, KD)
            pe.wait_ge(taken, TAKEN["p1"] + 2)
            group("v1", memT_hi, memT_lo, 0, 5)
            attend(0)
            group("v1", memT_hi, memT_lo, 5, KD)
            pe.wait_ge(taken, TAKEN["pv0"] + 4)
            group("xo0", yT_hi, yT_lo, 0, 5)
            attend(1)
            group("xo0", yT_hi, yT_lo, 5, 8)
            pe.wait_ge(taken, TAKEN["pv1"] + 4)
            group("xo0", yT_hi, yT_lo, 8, KD)
            resid("xo0", 0, "xo1", yT_hi, yT_lo, TAKEN["pv1"] + 4)
            group("xo1", yT_hi, yT_lo, 8, KD)
            resid("xo1", 1, "ffn2_in0", xT_hi, xT_lo, TAKEN["xo0"] + 4)
            pe.wait_ge(taken, TAKEN["xo1"] + 4)
            group("ffn2_in0", xT_hi, xT_lo, 8, KD)
            ffn_in(2)
            ffn_out(2)


_INS = ["x", "mem", "g_ffn1", "w_ffn1_in", "w_ffn1_out", "g_mix", "w_mix_in", "conv_w", "conv_b", "g_gm_v", "w_spatial",
        "b_spatial", "w_mix_out", "g_xattn", "g_mem", "w_xq", "w_xk", "w_xv", "w_xo", "g_ffn2", "w_ffn2_in",
        "w_ffn2_out", "g_final"]


def kernel(**inputs):
    import numpy as np
    import concourse.bacc as bacc
    from concourse.bass_utils import run_bass_kernel_spmd

    nc = bacc.Bacc("TRN2", target_bir_lowering=False, num_devices=1)
    arrays, args = {}, []
    for name in _INS:
        a = np.ascontiguousarray(inputs[name])
        arrays[f"in_{name}"] = a
        args.append(nc.dram_tensor(f"in_{name}", a.shape, mybir.dt.from_np(a.dtype), kind="ExternalInput").ap())
    shape = arrays["in_x"].shape
    args.append(nc.dram_tensor("out_0", shape, F32, kind="ExternalOutput").ap())
    build(nc, *args)
    r = run_bass_kernel_spmd(nc, [arrays], core_ids=[0])
    return r.results[0]["out_0"]
```

```python
from contextlib import ExitStack

import concourse.bass as bass
from concourse import mybir

ALU = mybir.AluOpType
ACT = mybir.ActivationFunctionType
AX_X = mybir.AxisListType.X
F32 = mybir.dt.float32
F32R = mybir.dt.float32r

P = 128
TOK = 2
SEQ = TOK * P
Q = 32
BLK = 512
GW = 2 * BLK
SETW = 4 * BLK
RAW = 4
RING = 4
LATE = 13
EPS = 1e-6
XA_HEADS = 4


def starts(steps):
    at, n = {}, 0
    for name, k in steps:
        at[name] = n
        n += k
    return at


def build(nc, x, mem, g_ffn1, w_ffn1_in, w_ffn1_out, g_mix, w_mix_in, conv_w, conv_b, g_gm_v, w_spatial, b_spatial,
          w_mix_out, g_xattn, g_mem, w_xq, w_xk, w_xv, w_xo, g_ffn2, w_ffn2_in, w_ffn2_out, g_final, out):
    D = x.shape[2]
    KD = D // P
    FF = w_ffn1_out.shape[1]
    KF = FF // P
    FG = FF // BLK
    HEADS = w_spatial.shape[1]
    HALF = GW // P
    HD = D // XA_HEADS
    DT = HD // P
    SCALE = float(HD) ** -0.5
    assert KD % RING == 0 and KF % RING == 0 and FG % 2 == 1 and D == 2 * GW and HEADS == HALF

    groups = [(f"ffn1_in{g}", KD) for g in range(FG)] + [("ffn1_out0", KF), ("ffn1_out1", KF)]
    groups += [(n, KD) for n in ("C", "H", "B", "V", "U", "mix_out0", "mix_out1", "q0", "q1", "k0", "k1", "v0", "v1",
                                 "xo0", "xo1")]
    groups += [(f"ffn2_in{g}", KD) for g in range(FG)] + [("ffn2_out0", KF), ("ffn2_out1", KF)]
    UNIT0 = starts(groups)
    UNITS = dict(groups)
    SET = {name: i % 2 for i, (name, _) in enumerate(groups)}

    def done(group):
        return UNIT0[group] + UNITS[group]

    f1 = [(f"ffn1_in{g}", 2) for g in range(FG)]
    f2 = [(f"ffn2_in{g}", 2) for g in range(FG)]
    TURN = starts([("x0", 4), ("x1", 4)] + f1 + [("ffn1_out0", 4), ("ffn1_out1", 4), ("ws", 2), ("H", 4), ("B", 4),
                  ("U", 4), ("mix_out0", 4), ("memA", 4), ("mix_out1", 4), ("memB", 4), ("q0", 4), ("q1", 4),
                  ("k0", 4), ("p0", 2), ("k1", 4), ("p1", 2), ("xo0", 4), ("xo1", 4)] + f2)
    HI = starts([("x0", 4), ("x1", 4)] + f1 + [("ffn1_out0", 4), ("ffn1_out1", 4), ("U", 4), ("mix_out0", 4),
                ("memA", 4), ("mix_out1", 4), ("memB", 4), ("q0", 4), ("q1", 4), ("k0", 4), ("p0", 2), ("k1", 4),
                ("p1", 2), ("pv0", 4), ("pv1", 4), ("xo0", 4), ("xo1", 4)] + f2)
    TAKEN = starts([("x0", 4), ("x1", 4)] + f1 + [("ffn1_out0", 4), ("ffn1_out1", 4), ("ws", 2), ("U", 4),
                   ("mix_out0", 4), ("memA", 4), ("mix_out1", 4), ("memB", 4), ("q0", 4), ("q1", 4), ("k0", 4),
                   ("p0", 2), ("k1", 4), ("p1", 2), ("pv0", 4), ("pv1", 4), ("xo0", 4), ("xo1", 4)] + f2)
    STAGED = starts([(f"ffn1_in{g}", 2) for g in range(FG)] + [(n, 2) for n in (
        "ffn1_out0", "ffn1_out1", "H", "B", "U", "mix_out0", "mix_out1", "q0", "q1", "k0", "k1", "xo0", "xo1")]
        + [(f"ffn2_in{g}", 2) for g in range(FG)] + [("ffn2_out0", 2), ("ffn2_out1", 2 * TOK)])
    SQUARED = starts([(n, 2) for n in ("x0", "x1", "ffn1_out0", "ffn1_out1", "mix_out0", "mix_out1", "mem0", "mem1",
                                       "xo0", "xo1", "ffn2_out0")] + [("ffn2_out1", 2 * TOK)])
    NORM = starts([(n, 1) for n in ("x", "ffn1", "v", "mix", "mem", "xo", "final0", "final1")])

    BASE = (nc.sbuf_base + 31) // 32 * 32
    KB = 1024
    place = {"at": BASE}

    def put(name, shape, dt, at=None):
        size = 4
        for s in shape[1:]:
            size *= s
        if at is None:
            at = place["at"]
            place["at"] = at + (size + 31) // 32 * 32
        return nc.alloc_sbuf_tensor_at(name, shape, dt, offset=at)

    h = put("h", [P, TOK, D], F32)
    xT_hi = put("xT_hi", [P, KD, SEQ], F32R)
    xT_lo = put("xT_lo", [P, KD, SEQ], F32R)
    raw = put("raw", [P, RAW, GW], F32)
    w_hi = put("w_hi", [P, RING, GW], F32R)
    w_lo = put("w_lo", [P, RING, GW], F32R)
    stage = put("stage", [P, TOK, GW], F32)
    scratch = put("scratch", [P, GW], F32)
    ident = put("ident", [P, P], F32)
    rows = put("rows", [P, P], F32)
    cols = put("cols", [P, P], F32)
    ssq = put("ssq", [P, 2, TOK], F32)
    ssq_end = put("ssq_end", [P, TOK, 2], F32)
    ms_part = put("ms_part", [P, TOK], F32)
    rstd = put("rstd", [P, TOK], F32)
    rstd_mem = put("rstd_mem", [P, TOK], F32)
    rstd_v = put("rstd_v", [P, TOK * HEADS], F32)
    ssv = put("ssv", [P, TOK * HEADS], F32)
    small = put("small", [P, 4, TOK * HEADS], F32)
    smax = put("smax", [P, 4], F32)
    nbias = put("nbias", [P, 4], F32)
    rsum = put("rsum", [P, 4], F32)
    rinv = put("rinv", [P, 4], F32)
    extra = place["at"]
    g_v = put("g_v", [P, GW], F32, at=extra)
    ws = put("ws", [P, HEADS, P], F32, at=extra + 4 * KB)
    pT_hi = put("pT_hi", [P, XA_HEADS * 2, SEQ], F32R, at=extra)
    g_fin = put("g_fin", [P, D], F32, at=extra)
    big = extra + 8 * KB
    hidT_hi = put("hidT_hi", [P, KF, SEQ], F32R, at=big)
    hidT_lo = put("hidT_lo", [P, KF, SEQ], F32R, at=big + KF * KB)
    yT_hi = put("yT_hi", [P, KD, SEQ], F32R, at=big)
    yT_lo = put("yT_lo", [P, KD, SEQ], F32R, at=big + 16 * KB)
    memT_hi = put("memT_hi", [P, KD, SEQ], F32R, at=big + 32 * KB)
    memT_lo = put("memT_lo", [P, KD, SEQ], F32R, at=big + 48 * KB)
    c_buf = put("c_buf", [P, TOK, GW], F32, at=big + 32 * KB)
    zT = put("zT", [P, HALF, SEQ], F32, at=big + 40 * KB)
    convT = put("convT", [P, HALF, SEQ], F32, at=big + 48 * KB)
    v_buf = put("v_buf", [P, TOK, GW], F32, at=big + 56 * KB)
    wsT = put("wsT", [P, HEADS, P], F32, at=big + 64 * KB)
    sg = put("sg", [P, TOK, GW], F32, at=big + 80 * KB)
    mem_nat = put("mem_nat", [P, TOK, D], F32, at=big + 64 * KB)
    v_hi = put("v_hi", [P, TOK, GW], F32R, at=big + 64 * KB)
    v_lo = put("v_lo", [P, TOK, GW], F32R, at=big + 72 * KB)
    pT_lo = put("pT_lo", [P, XA_HEADS * 2, SEQ], F32R, at=big + 80 * KB)
    qT_hi, qT_lo = yT_hi, yT_lo
    kT_hi, kT_lo = xT_hi, xT_lo
    assert big + 2 * KF * KB <= nc.sbuf_usable_end

    vectors = [("g_ffn1", g_ffn1[0], KD), ("g_mix", g_mix[0], KD), ("g_xattn", g_xattn[0], KD), ("g_mem", g_mem[0], KD),
               ("g_ffn2", g_ffn2[0], KD), ("conv_w", conv_w[0].rearrange("k c -> (k c)"), 3 * HALF),
               ("conv_b", conv_b[0], HALF), ("b_spatial", b_spatial[0].rearrange("h t -> (h t)"), HEADS)]
    ROW = starts([(n, k) for n, _, k in vectors])
    NROWS = sum(k for _, _, k in vectors)

    def col(name, k):
        return cols[:, ROW[name] + k:ROW[name] + k + 1]

    with ExitStack() as ctx:
        def sem(name):
            return ctx.enter_context(nc.semaphore(name))

        ps = ctx.enter_context(nc.psum_tensor("ps", [P, 2 * SETW], F32))

        def bank(s, c0, n):
            return ps[:, s * SETW + c0:s * SETW + c0 + n]

        raw_loaded = [sem(f"raw_loaded{i}") for i in range(RAW)]
        hi_ready = sem("hi_ready")
        lo_ready = sem("lo_ready")
        unit_used = sem("unit_used")
        staged = sem("staged")
        turned = sem("turned")
        hi_taken = sem("hi_taken")
        taken = sem("taken")
        silu_ready = sem("silu_ready")
        squared = sem("squared")
        ms_ready = sem("ms_ready")
        root_ready = sem("root_ready")
        rstd_ready = sem("rstd_ready")
        dve_step = sem("dve_step")
        act_step = sem("act_step")
        x_loaded = [sem(f"x_loaded{i}") for i in range(D // BLK)]
        gain_loaded = sem("gain_loaded")
        rows_loaded = sem("rows_loaded")
        gv_loaded = sem("gv_loaded")
        ws_loaded = sem("ws_loaded")
        mem_loaded = sem("mem_loaded")
        gfin_loaded = sem("gfin_loaded")
        ident_zero = sem("ident_zero")
        ident_ready = sem("ident_ready")
        ws_masked = sem("ws_masked")
        rows_turned = sem("rows_turned")
        cols_ready = sem("cols_ready")
        c_taken = sem("c_taken")
        z_taken = sem("z_taken")
        conv_done = sem("conv_done")
        yc_product = sem("yc_product")
        yc_hi = sem("yc_hi")
        yc_ready = sem("yc_ready")
        v_squared = sem("v_squared")
        vn_ready = sem("vn_ready")
        gated = sem("gated")
        sg_ready = sem("sg_ready")
        scored = sem("scored")
        nbias_ready = sem("nbias_ready")
        exp_ready = sem("exp_ready")
        probs_ready = sem("probs_ready")
        v_rounded = sem("v_rounded")
        v_split = sem("v_split")
        pv_done = sem("pv_done")
        last_block = sem("last_block")
        gained = sem("gained")
        out_ready = [sem(f"out_ready{c}") for c in range(2)]
        out_stored = sem("out_stored")

        block = ctx.enter_context(nc.Block())

        def ffn_in_src(w, col0):
            v = w[0].rearrange("(k p) (s n) -> k p s n", p=P, s=2)
            return lambda k: v[k][:, :, bass.ds(col0, BLK)]

        def cols_src(w, col0):
            v = w[0].rearrange("(k p) n -> k p n", p=P)
            return lambda k: v[k][:, col0:col0 + GW]

        @block.sync
        def _(sp):
            def load_units(src, unit0, n, k0=0):
                for k in range(k0, n):
                    dst = raw[:, k % RAW, :]
                    if len(src(k).shape) == 3:
                        dst = dst.rearrange("p (s n) -> p s n", s=2)
                    if not (isinstance(unit0, int) and unit0 + k < RAW):
                        sp.wait_ge(lo_ready, unit0 + (k - RAW + 1))
                    sp.dma_start(dst, src(k)).then_inc(raw_loaded[k % RAW], 16)

            def load_ffn_in(f, w, k0=0):
                u0 = UNIT0[f"ffn{f}_in0"]
                load_units(ffn_in_src(w, 0), u0, KD, k0)
                with sp.Fori(0, FG // 2) as i:
                    for j in range(2):
                        load_units(ffn_in_src(w, i * GW + (1 + j) * BLK), i * (2 * KD) + (u0 + (1 + j) * KD), KD)

            def load_pair(name, w, n):
                for c in range(2):
                    load_units(cols_src(w, c * GW), UNIT0[f"{name}{c}"], n)

            xv = x[0].rearrange("(t p) n -> p t n", p=P)
            first = ffn_in_src(w_ffn1_in, 0)

            def load_x(c):
                sp.dma_start(h[:, :, c * BLK:(c + 1) * BLK], xv[:, :, c * BLK:(c + 1) * BLK]).then_inc(x_loaded[c], 16)

            load_x(0)
            load_units(first, 0, 1)
            load_x(1)
            load_units(first, 0, 4, 1)
            load_x(2)
            load_x(3)
            load_ffn_in(1, w_ffn1_in, RAW)
            load_pair("ffn1_out", w_ffn1_out, KF)
            for name, c in (("C", 1), ("H", 2), ("B", 0), ("V", 4), ("U", 3)):
                load_units(cols_src(w_mix_in, c * GW), UNIT0[name], KD)
            sp.wait_ge(gated, 4)
            sp.dma_start(mem_nat[:, :, :], mem[0].rearrange("(t p) n -> p t n", p=P)).then_inc(mem_loaded, 16)
            load_pair("mix_out", w_mix_out, KD)
            load_pair("q", w_xq, KD)
            load_pair("k", w_xk, KD)
            load_pair("v", w_xv, KD)
            load_pair("xo", w_xo, KD)
            sp.wait_ge(pv_done, 8)
            sp.dma_start(g_fin[:, :], g_final.partition_broadcast(P)).then_inc(gfin_loaded, 16)
            load_ffn_in(2, w_ffn2_in)
            load_pair("ffn2_out", w_ffn2_out, KF)
            ov = out[0].rearrange("(t p) n -> p t n", p=P)
            for t in range(TOK):
                for c in range(2):
                    sp.wait_ge(out_ready[c], t + 1)
                    sp.dma_start(ov[:, t, c * GW:(c + 1) * GW], h[:, t, c * GW:(c + 1) * GW]).then_inc(out_stored, 16)
            sp.wait_ge(out_stored, 16 * TOK * 2)

        @block.gpsimd
        def _(pool):
            pool.memset(ident[:, :], 0.0).then_inc(ident_zero, 1)
            pool.wait_ge(ident_zero, 1)
            pool.affine_select(out=ident[:, :], in_=ident[:, :], compare_op=ALU.not_equal, fill=1.0, base=0,
                               pattern=[[-1, P]], channel_multiplier=1).then_inc(ident_ready, 1)
            pool.wait_ge(ws_loaded, 16)
            pool.affine_select(out=ws[:, :, :], in_=ws[:, :, :], compare_op=ALU.is_ge, fill=0.0, base=0,
                               pattern=[[0, HEADS], [-1, P]], channel_multiplier=1).then_inc(ws_masked, 1)

        @block.scalar
        def _(act):
            def hi_units(unit0, k0, k1):
                for k in range(k0, k1):
                    act.wait_ge(raw_loaded[k % RAW], unit0 * (16 // RAW) + 16 * (k // RAW + 1))
                    if not (isinstance(unit0, int) and unit0 + k < RING):
                        act.wait_ge(unit_used, unit0 + (k - RING + 1))
                    nc.scalar.activation(w_hi[:, k % RING, :], raw[:, k % RAW, :], ACT.Copy).then_inc(hi_ready, 1)

            def hi_scaled(dst, k0, g, s, name, b0=0, b1=4):
                for b in range(b0, b1):
                    act.wait_ge(turned, TURN[name] + b + 1)
                    for j in range(2):
                        k = 2 * b + j
                        ins = nc.scalar.activation(dst[:, k0 + k, :], bank(s, k * SEQ, SEQ), ACT.Copy, scale=col(g, k0 + k))
                    ins.then_inc(hi_taken, 1)

            def hi_plain(dst, k0, s, banks, ready, first, b0=0):
                for b in range(banks):
                    act.wait_ge(ready, first + b + 1)
                    nc.scalar.activation(dst[:, bass.ds(k0 + 2 * b, 2), :].rearrange("p k t -> p (k t)"),
                                         bank(s, (b0 + b) * BLK, BLK), ACT.Copy).then_inc(hi_taken, 1)

            def squares(src, c, name):
                for t in range(TOK):
                    if SQUARED[name] + t > 0:
                        act.wait_ge(squared, SQUARED[name] + t)
                    nc.scalar.activation(scratch[:, :], src[:, t, c * GW:(c + 1) * GW], ACT.Square,
                                         accum_out=ssq[:, c, t:t + 1]).then_inc(squared, 1)

            def root(norm, n):
                act.wait_ge(ms_ready, NORM[norm] + 1)
                nc.scalar.activation(small[:, 1, 0:n], small[:, 0, 0:n], ACT.Sqrt).then_inc(root_ready, 1)

            def silu(s, used):
                act.wait_ge(unit_used, used)
                for t in range(TOK):
                    nc.scalar.activation(scratch[:, t * BLK:(t + 1) * BLK], bank(s, t * GW, BLK), ACT.Silu,
                                         scale=rstd[:, t:t + 1]).then_inc(silu_ready, 1)

            def resid(name, c, dst, g, first, half, at=8):
                hi_units(first, 0, 4)
                act.wait_ge(staged, STAGED[name] + TOK)
                squares(h, c, name)
                hi_units(first, 4, at)
                hi_scaled(dst, c * HALF, g, half, name)

            def ffn_in(f, norm):
                u0 = UNIT0[f"ffn{f}_in0"]
                act.wait_ge(rstd_ready, NORM[norm] + 1)
                with act.Fori(0, FG // 2) as i:
                    for j in range(2):
                        unit0 = i * (2 * KD) + (u0 + (1 + j) * KD)
                        hi_units(unit0, 0, 4)
                        silu(j, unit0)
                        hi_units(unit0, 4, 11)
                        hi_plain(hidT_hi, i * 8 + 4 * j, j, 2, turned, i * 4 + (TURN[f"ffn{f}_in0"] + 2 * j))
                        hi_units(unit0, 11, KD)

            def ffn_out(f):
                last = f"ffn{f}_in{FG - 1}"
                u0 = UNIT0[f"ffn{f}_out0"]
                hi_units(u0, 0, 4)
                silu(SET[last], u0)
                hi_units(u0, 4, 11)
                hi_plain(hidT_hi, 4 * (FG - 1), SET[last], 2, turned, TURN[last])
                hi_units(u0, 11, KF)

            def load_rows(name, v, k, landed):
                act.dma_start(rows[ROW[name]:ROW[name] + k, :], v.rearrange("(r c) -> r c", c=P)).then_inc(landed, 16)

            load_rows(*vectors[0], gain_loaded)
            act.wait_ge(ident_ready, 1)
            nc.scalar.activation(small[:, 3, 0:1], ident[:, 0:1], ACT.Copy)
            act.wait_ge(cols_ready, 1)
            for b in range(2):
                hi_scaled(xT_hi, 0, "g_ffn1", 1, "x0", b, b + 1)
                hi_units(0, b, b + 1)
            hi_units(0, 2, 3)
            hi_scaled(xT_hi, 0, "g_ffn1", 1, "x0", 2, 4)
            hi_units(0, 3, 4)
            squares(h, 0, "x0")
            hi_units(0, 4, 5)
            hi_scaled(xT_hi, HALF, "g_ffn1", 1, "x1", 0, 2)
            hi_units(0, 5, 7)
            hi_scaled(xT_hi, HALF, "g_ffn1", 1, "x1", 2, 4)
            hi_units(0, 7, 9)
            for v in vectors[1:]:
                load_rows(*v, rows_loaded)
            hi_units(0, 9, 11)
            squares(h, 1, "x1")
            hi_units(0, 11, 13)
            root("x", TOK)
            hi_units(0, 13, KD)
            act.dma_start(ws[:, :, :], w_spatial[0].rearrange("h t s -> t h s")).then_inc(ws_loaded, 16)
            act.dma_start(g_v[:, :], g_gm_v[0].partition_broadcast(P)).then_inc(gv_loaded, 16)
            ffn_in(1, "x")
            ffn_out(1)
            u = UNIT0["ffn1_out1"]
            resid("ffn1_out0", 0, xT_hi, "g_mix", u, SET["ffn1_out0"], LATE)
            hi_units(u, LATE, KF)
            u = UNIT0["C"]
            resid("ffn1_out1", 1, xT_hi, "g_mix", u, SET["ffn1_out1"])
            root("ffn1", TOK)
            hi_units(u, 8, KD)
            u = UNIT0["H"]
            hi_units(u, 0, 4)
            act.wait_ge(unit_used, done("C"))
            act.wait_ge(rstd_ready, NORM["ffn1"] + 1)
            for t in range(TOK):
                nc.scalar.activation(c_buf[:, t, :], bank(SET["C"], t * GW, GW), ACT.Copy,
                                     scale=rstd[:, t:t + 1]).then_inc(c_taken, 1)
            hi_units(u, 4, KD)
            u = UNIT0["B"]
            hi_units(u, 0, LATE)
            for b in range(4):
                act.wait_ge(turned, TURN["H"] + b + 1)
                nc.scalar.activation(zT[:, 2 * b:2 * b + 2, :].rearrange("p k t -> p (k t)"), bank(SET["H"], b * BLK, BLK),
                                     ACT.Copy)
                for k in (2 * b, 2 * b + 1):
                    nc.scalar.activation(convT[:, k, :], bank(SET["H"], k * SEQ, SEQ), ACT.Identity,
                                         scale=col("conv_w", 2 * HALF + k), bias=col("conv_b", k)).then_inc(z_taken, 1)
            hi_units(u, LATE, KD)
            u = UNIT0["V"]
            hi_units(u, 0, LATE + 1)
            act.wait_ge(yc_product, 1)
            nc.scalar.activation(yT_hi[:, 0:HALF, :], convT[:, :, :], ACT.Copy).then_inc(yc_hi, 1)
            hi_units(u, LATE + 1, KD)
            u = UNIT0["U"]
            hi_units(u, 0, 4)
            act.wait_ge(unit_used, done("V"))
            for t in range(TOK):
                nc.scalar.activation(v_buf[:, t, :], bank(SET["V"], t * GW, GW), ACT.Copy,
                                     scale=rstd[:, t:t + 1]).then_inc(act_step, 1)
            act.wait_ge(act_step, TOK)
            act.wait_ge(staged, STAGED["H"] + TOK)
            nc.scalar.activation(c_buf[:, :, :], v_buf[:, :, :], ACT.Square).then_inc(v_squared, 1)
            hi_units(u, 4, 7)
            root("v", TOK * HEADS)
            hi_units(u, 7, 14)
            for hd in range(HEADS):
                if hd % 2 == 0:
                    act.wait_ge(gated, hd // 2 + 1)
                nc.scalar.activation(sg[:, :, hd * P:(hd + 1) * P],
                                     bank(SET["V"], hd * SEQ, SEQ).rearrange("p (t c) -> p t c", t=TOK), ACT.Identity,
                                     bias=col("b_spatial", hd)).then_inc(sg_ready, 1)
            hi_units(u, 14, KD)
            u = UNIT0["mix_out0"]
            hi_units(u, 0, 8)
            hi_plain(yT_hi, HALF, SET["U"], 4, turned, TURN["U"])
            hi_units(u, 8, KD)
            u = UNIT0["mix_out1"]
            resid("mix_out0", 0, xT_hi, "g_xattn", u, SET["mix_out0"])
            hi_units(u, 8, 13)
            hi_scaled(memT_hi, 0, "g_mem", SET["mix_out0"], "memA")
            hi_units(u, 13, KD)
            u = UNIT0["q0"]
            resid("mix_out1", 1, xT_hi, "g_xattn", u, SET["mix_out1"])
            root("mix", TOK)
            hi_units(u, 8, 13)
            hi_scaled(memT_hi, HALF, "g_mem", SET["mix_out1"], "memB")
            hi_units(u, 13, KD)
            u = UNIT0["q1"]
            hi_units(u, 0, 4)
            for c in range(2):
                squares(mem_nat, c, f"mem{c}")
            hi_units(u, 4, LATE)
            root("mem", TOK)
            hi_plain(qT_hi, 0, SET["q0"], 4, turned, TURN["q0"])
            hi_units(u, LATE, KD)
            u = UNIT0["k0"]
            hi_units(u, 0, LATE)
            hi_plain(qT_hi, HALF, SET["q1"], 4, turned, TURN["q1"])
            hi_units(u, LATE, KD)
            for pair, running in enumerate(("k1", "v0")):
                u = UNIT0[running]
                s = SET[f"k{pair}"]
                hi_units(u, 0, 8)
                hi_plain(kT_hi, pair * HALF, s, 4, turned, TURN[f"k{pair}"])
                hi_units(u, 8, 11)
                act.wait_ge(nbias_ready, pair + 1)
                for j in range(4):
                    nc.scalar.activation(scratch[:, j * SEQ:(j + 1) * SEQ], bank(s, j * SEQ, SEQ), ACT.Exp,
                                         bias=nbias[:, j:j + 1], scale=SCALE, accum_out=rsum[:, j:j + 1]
                                         ).then_inc(exp_ready, 1)
                hi_units(u, 11, 15)
                hi_plain(pT_hi, 4 * pair, s, 2, turned, TURN[f"p{pair}"], b0=2)
                hi_units(u, 15, KD)
            for pair, running in enumerate(("v1", "xo0")):
                u = UNIT0[running]
                s = SET[f"v{pair}"]
                hi_units(u, 0, 4)
                act.wait_ge(unit_used, done(f"v{pair}"))
                act.wait_ge(rstd_ready, NORM["mem"] + 1)
                for t in range(TOK):
                    nc.scalar.activation(v_hi[:, t, :], bank(s, t * GW, GW), ACT.Copy,
                                         scale=rstd_mem[:, t:t + 1]).then_inc(v_rounded, 1)
                hi_units(u, 4, 9)
                hi_plain(yT_hi, pair * HALF, s, 4, pv_done, 4 * pair)
                hi_units(u, 9, KD)
            u = UNIT0["xo1"]
            resid("xo0", 0, xT_hi, "g_ffn2", u, SET["xo0"], LATE)
            hi_units(u, LATE, KD)
            u = UNIT0["ffn2_in0"]
            resid("xo1", 1, xT_hi, "g_ffn2", u, SET["xo1"])
            root("xo", TOK)
            hi_units(u, 8, KD)
            ffn_in(2, "xo")
            ffn_out(2)
            u = UNIT0["ffn2_out1"]
            hi_units(u, 0, 4)
            act.wait_ge(staged, STAGED["ffn2_out0"] + TOK)
            squares(h, 0, "ffn2_out0")
            hi_units(u, 4, KF)
            for t in range(TOK):
                for b in range(2):
                    n = 2 * t + b
                    act.wait_ge(staged, STAGED["ffn2_out1"] + n + 1)
                    act.wait_ge(squared, SQUARED["ffn2_out1"] + n)
                    nc.scalar.activation(scratch[:, 0:BLK], h[:, t, GW + b * BLK:GW + (b + 1) * BLK], ACT.Square,
                                         accum_out=ssq_end[:, t, b:b + 1]).then_inc(squared, 1)
                root(f"final{t}", 1)
                act.wait_ge(gained, TOK + 2 * t + 2)
                act.wait_ge(rstd_ready, NORM[f"final{t}"] + 1)
                nc.scalar.activation(h[:, t, GW:D], stage[:, t, :], ACT.Copy, scale=rstd[:, t:t + 1]).then_inc(out_ready[1], 1)

        @block.vector
        def _(dve):
            steps = [0]

            def chain(ins):
                ins.then_inc(dve_step, 1)
                steps[0] += 1
                dve.wait_ge(dve_step, steps[0])

            def lo_units(unit0, k0, k1):
                for k in range(k0, k1):
                    dve.wait_ge(hi_ready, unit0 + (k + 1))
                    nc.vector.tensor_tensor(w_lo[:, k % RING, :], raw[:, k % RAW, :], w_hi[:, k % RING, :].bitcast(F32),
                                            ALU.subtract).then_inc(lo_ready, 1)

            def lo_scaled(dst, hi, k0, g, s, name, b0=0, b1=4):
                for b in range(b0, b1):
                    dve.wait_ge(hi_taken, HI[name] + b + 1)
                    for j in range(2):
                        k = 2 * b + j
                        ins = nc.vector.scalar_tensor_tensor(out=dst[:, k0 + k, :], in0=bank(s, k * SEQ, SEQ),
                                                             scalar=col(g, k0 + k), in1=hi[:, k0 + k, :].bitcast(F32),
                                                             op0=ALU.mult, op1=ALU.subtract)
                    ins.then_inc(taken, 1)

            def lo_plain(dst, hi, k0, s, banks, first, b0=0):
                for b in range(banks):
                    dve.wait_ge(hi_taken, first + b + 1)
                    nc.vector.tensor_tensor(dst[:, bass.ds(k0 + 2 * b, 2), :].rearrange("p k t -> p (k t)"),
                                            bank(s, (b0 + b) * BLK, BLK),
                                            hi[:, bass.ds(k0 + 2 * b, 2), :].rearrange("p k t -> p (k t)").bitcast(F32),
                                            ALU.subtract).then_inc(taken, 1)

            def norm(name, total, count, res):
                ms, rt, inv, t = (small[:, i, 0:res.shape[1]] for i in range(4))
                if isinstance(total, tuple):
                    chain(nc.vector.tensor_tensor(t, total[0], total[1], ALU.add))
                    total = t
                nc.vector.tensor_scalar(ms, total, 1.0 / count, EPS, ALU.mult, ALU.add).then_inc(ms_ready, 1)
                dve.wait_ge(root_ready, NORM[name] + 1)
                chain(nc.vector.reciprocal(inv, rt))
                chain(nc.vector.tensor_tensor(t, inv, inv, ALU.mult))
                chain(nc.vector.tensor_tensor(t, t, ms, ALU.mult))
                chain(nc.vector.tensor_scalar(t, t, -0.5, 1.5, ALU.mult, ALU.add))
                nc.vector.tensor_tensor(res, inv, t, ALU.mult).then_inc(rstd_ready, 1)
                dve.wait_ge(rstd_ready, NORM[name] + 1)

            def add_resid(name, c, coef):
                dve.wait_ge(unit_used, done(name))
                for t in range(TOK):
                    hs = h[:, t, c * GW:(c + 1) * GW]
                    nc.vector.scalar_tensor_tensor(out=hs, in0=bank(SET[name], t * GW, GW), scalar=coef, in1=hs,
                                                   op0=ALU.mult, op1=ALU.add).then_inc(staged, 1)

            def resid(name, c, coef, g, first, by_dve=False):
                lo_units(first, 0, 4)
                add_resid(name, c, coef)
                if by_dve:
                    turn_between(name, h[:, :, c * GW:(c + 1) * GW], first)
                else:
                    lo_units(first, 4, 8)
                lo_scaled(xT_lo, xT_hi, c * HALF, g, SET[name], name)

            def turn_blocks(src, s, tiles, n0, n1):
                dst = bank(s, 0, tiles * SEQ).rearrange("p (k t b) -> p t k b", t=TOK, b=P)
                src = src.rearrange("p t (k c) -> p t k c", c=P)
                for n in range(n0, n1):
                    q, j = n // 4, n % 4
                    ins = nc.vector.transpose(dst[j * Q:(j + 1) * Q, :, :, q * Q:(q + 1) * Q],
                                              src[q * Q:(q + 1) * Q, :, :, j * Q:(j + 1) * Q])
                    if n == 15:
                        ins.then_inc(turned, tiles // 2)

            def turn_between(name, src, u):
                lo_units(u, 4, 5)
                dve.wait_ge(staged, STAGED[name] + TOK)
                for i in range(8):
                    turn_blocks(src, SET[name], HALF, 2 * i, 2 * i + 2)
                    lo_units(u, 5 + i, 6 + i)

            def gate(s, silus):
                for t in range(TOK):
                    dve.wait_ge(silu_ready, silus + t + 1)
                    nc.vector.scalar_tensor_tensor(out=stage[:, t, 0:BLK], in0=bank(s, t * GW + BLK, BLK),
                                                   scalar=rstd[:, t:t + 1], in1=scratch[:, t * BLK:(t + 1) * BLK],
                                                   op0=ALU.mult, op1=ALU.mult).then_inc(staged, 1)

            def ffn_in(f):
                u0 = UNIT0[f"ffn{f}_in0"]
                s0 = (f - 1) * 2 * FG
                with dve.Fori(0, FG // 2) as i:
                    for j in range(2):
                        unit0 = i * (2 * KD) + (u0 + (1 + j) * KD)
                        lo_units(unit0, 0, 4)
                        gate(j, i * 4 + (s0 + 2 * j))
                        lo_units(unit0, 4, 5)
                        dve.wait_ge(staged, i * 4 + (STAGED[f"ffn{f}_in0"] + 2 * j + TOK))
                        for q in range(4):
                            turn_blocks(stage[:, :, 0:BLK], j, BLK // P, 4 * q, 4 * q + 4)
                            lo_units(unit0, 5 + q, 6 + q)
                        lo_units(unit0, 9, 11)
                        lo_plain(hidT_lo, hidT_hi, i * 8 + 4 * j, j, 2, i * 4 + (HI[f"ffn{f}_in0"] + 2 * j))
                        lo_units(unit0, 11, KD)

            def ffn_out(f):
                last = f"ffn{f}_in{FG - 1}"
                u0 = UNIT0[f"ffn{f}_out0"]
                lo_units(u0, 0, 4)
                gate(SET[last], (f - 1) * 2 * FG + 2 * (FG - 1))
                lo_units(u0, 4, 5)
                dve.wait_ge(staged, STAGED[last] + TOK)
                for q in range(4):
                    turn_blocks(stage[:, :, 0:BLK], SET[last], BLK // P, 4 * q, 4 * q + 4)
                    lo_units(u0, 5 + q, 6 + q)
                lo_units(u0, 9, 11)
                lo_plain(hidT_lo, hidT_hi, 4 * (FG - 1), SET[last], 2, HI[last])
                lo_units(u0, 11, KF)

            def scaled(name, scale):
                dve.wait_ge(unit_used, done(name))
                for t in range(TOK):
                    nc.vector.tensor_scalar(stage[:, t, :], bank(SET[name], t * GW, GW), scale[:, t:t + 1], None,
                                            ALU.mult).then_inc(staged, 1)

            halves = (ssq[:, 0, :], ssq[:, 1, :])
            dve.wait_ge(rows_turned, 1)
            nc.vector.tensor_copy(cols[:, 0:KD], bank(0, 0, KD)).then_inc(cols_ready, 1)
            dve.wait_ge(cols_ready, 1)
            for b in range(2):
                lo_scaled(xT_lo, xT_hi, 0, "g_ffn1", 1, "x0", b, b + 1)
                lo_units(0, b, b + 1)
            lo_units(0, 2, 3)
            lo_scaled(xT_lo, xT_hi, 0, "g_ffn1", 1, "x0", 2, 4)
            lo_units(0, 3, 5)
            lo_scaled(xT_lo, xT_hi, HALF, "g_ffn1", 1, "x1", 0, 2)
            lo_units(0, 5, 7)
            lo_scaled(xT_lo, xT_hi, HALF, "g_ffn1", 1, "x1", 2, 4)
            lo_units(0, 7, 12)
            dve.wait_ge(squared, SQUARED["x1"] + 2)
            norm("x", halves, D, rstd[:, :])
            lo_units(0, 12, 14)
            dve.wait_ge(rows_turned, 2)
            nc.vector.tensor_copy(cols[:, KD:NROWS], bank(1, KD, NROWS - KD)).then_inc(cols_ready, 1)
            dve.wait_ge(cols_ready, 2)
            lo_units(0, 14, KD)
            ffn_in(1)
            ffn_out(1)
            u = UNIT0["ffn1_out1"]
            resid("ffn1_out0", 0, 0.5, "g_mix", u, by_dve=True)
            lo_units(u, LATE, KF)
            u = UNIT0["C"]
            resid("ffn1_out1", 1, 0.5, "g_mix", u)
            dve.wait_ge(squared, SQUARED["ffn1_out1"] + 2)
            norm("ffn1", halves, D, rstd[:, :])
            lo_units(u, 8, 13)
            for b in range(2):
                dve.wait_ge(turned, TURN["ws"] + b + 1)
                nc.vector.tensor_copy(wsT[:, 4 * b:4 * b + 4, :].rearrange("s h t -> s (h t)"),
                                      bank(SET["ffn1_out1"], b * BLK, BLK)).then_inc(taken, 1)
            lo_units(u, 13, KD)
            lo_units(UNIT0["H"], 0, KD)
            u = UNIT0["B"]
            lo_units(u, 0, 4)
            dve.wait_ge(unit_used, done("H"))
            for t in range(TOK):
                dve.wait_ge(c_taken, t + 1)
                nc.vector.scalar_tensor_tensor(out=stage[:, t, :], in0=bank(SET["H"], t * GW, GW), scalar=rstd[:, t:t + 1],
                                               in1=c_buf[:, t, :], op0=ALU.mult, op1=ALU.mult).then_inc(staged, 1)
            turn_between("H", stage[:, :, :], u)
            lo_units(u, LATE, KD)
            u = UNIT0["V"]
            dve.wait_ge(z_taken, HALF)
            for shift in (1, 2):
                for k in range(HALF):
                    y = convT[:, k, shift:SEQ]
                    nc.vector.scalar_tensor_tensor(out=y, in0=zT[:, k, 0:SEQ - shift],
                                                   scalar=col("conv_w", (2 - shift) * HALF + k), in1=y,
                                                   op0=ALU.mult, op1=ALU.add).then_inc(conv_done, 1)
                dve.wait_ge(conv_done, HALF * shift)
            lo_units(u, 0, 4)
            scaled("B", rstd)
            turn_between("B", stage[:, :, :], u)
            cv = convT[:, :, :].rearrange("p k t -> p (k t)")
            dve.wait_ge(turned, TURN["B"] + 4)
            nc.vector.tensor_tensor(cv, cv, bank(SET["B"], 0, SETW), ALU.mult).then_inc(yc_product, 1)
            lo_units(u, LATE, LATE + 2)
            dve.wait_ge(yc_product, 1)
            dve.wait_ge(yc_hi, 1)
            nc.vector.tensor_tensor(yT_lo[:, 0:HALF, :], convT[:, :, :], yT_hi[:, 0:HALF, :].bitcast(F32),
                                    ALU.subtract).then_inc(yc_ready, 1)
            lo_units(u, LATE + 2, KD)
            u = UNIT0["U"]
            lo_units(u, 0, 6)
            dve.wait_ge(v_squared, 1)
            chain(nc.vector.tensor_reduce(ssv[:, :], c_buf[:, :, :].rearrange("p t (h c) -> p (t h) c", c=P), AX_X, ALU.add))
            norm("v", ssv[:, :], P, rstd_v[:, :])
            vv = v_buf[:, :, :].rearrange("p t (h c) -> p (t h) c", c=P)
            chain(nc.vector.tensor_tensor(vv, vv, rstd_v[:, :].unsqueeze(2).to_broadcast([P, TOK * HEADS, P]), ALU.mult))
            lo_units(u, 6, 8)
            dve.wait_ge(gv_loaded, 16)
            for t in range(TOK):
                nc.vector.tensor_tensor(v_buf[:, t, :], v_buf[:, t, :], g_v[:, :], ALU.mult).then_inc(vn_ready, 1)
            lo_units(u, 8, KD)
            u = UNIT0["mix_out0"]
            lo_units(u, 0, 4)
            dve.wait_ge(unit_used, done("U"))
            dve.wait_ge(sg_ready, HEADS)
            for t in range(TOK):
                nc.vector.scalar_tensor_tensor(out=stage[:, t, :], in0=bank(SET["U"], t * GW, GW), scalar=rstd[:, t:t + 1],
                                               in1=sg[:, t, :], op0=ALU.mult, op1=ALU.mult).then_inc(staged, 1)
            lo_units(u, 4, 8)
            lo_plain(yT_lo, yT_hi, HALF, SET["U"], 4, HI["U"])
            lo_units(u, 8, KD)
            u = UNIT0["mix_out1"]
            resid("mix_out0", 0, 1.0, "g_xattn", u)
            lo_units(u, 8, 13)
            lo_scaled(memT_lo, memT_hi, 0, "g_mem", SET["mix_out0"], "memA")
            lo_units(u, 13, KD)
            u = UNIT0["q0"]
            resid("mix_out1", 1, 1.0, "g_xattn", u)
            dve.wait_ge(squared, SQUARED["mix_out1"] + 2)
            norm("mix", halves, D, rstd[:, :])
            lo_units(u, 8, 13)
            lo_scaled(memT_lo, memT_hi, HALF, "g_mem", SET["mix_out1"], "memB")
            lo_units(u, 13, KD)

            for c, running in enumerate(("q1", "k0")):
                u = UNIT0[running]
                lo_units(u, 0, 4)
                scaled(f"q{c}", rstd)
                turn_between(f"q{c}", stage[:, :, :], u)
                if c == 0:
                    dve.wait_ge(squared, SQUARED["mem1"] + 2)
                    norm("mem", halves, D, rstd_mem[:, :])
                lo_plain(qT_lo, qT_hi, c * HALF, SET[f"q{c}"], 4, HI[f"q{c}"])
                lo_units(u, LATE, KD)
            for pair, running in enumerate(("k1", "v0")):
                u = UNIT0[running]
                name = f"k{pair}"
                lo_units(u, 0, 4)
                scaled(name, rstd_mem)
                lo_units(u, 4, 8)
                lo_plain(kT_lo, kT_hi, pair * HALF, SET[name], 4, HI[name])
                lo_units(u, 8, 11)
                dve.wait_ge(scored, pair + 1)
                chain(nc.vector.tensor_reduce(smax[:, :], bank(SET[name], 0, GW).rearrange("p (j m) -> p j m", j=4),
                                              AX_X, ALU.max))
                nc.vector.tensor_scalar(nbias[:, :], smax[:, :], -SCALE, None, ALU.mult).then_inc(nbias_ready, 1)
                dve.wait_ge(exp_ready, 4 * (pair + 1))
                chain(nc.vector.reciprocal(rinv[:, :], rsum[:, :]))
                pv = scratch[:, :].rearrange("p (j m) -> p j m", j=4)
                nc.vector.tensor_tensor(pv, pv, rinv[:, :].unsqueeze(2).to_broadcast([P, 4, SEQ]),
                                        ALU.mult).then_inc(probs_ready, 1)
                lo_units(u, 11, 15)
                lo_plain(pT_lo, pT_hi, 4 * pair, SET[name], 2, HI[f"p{pair}"], b0=2)
                lo_units(u, 15, KD)
            for pair, running in enumerate(("v1", "xo0")):
                u = UNIT0[running]
                s = SET[f"v{pair}"]
                lo_units(u, 0, 4)
                for t in range(TOK):
                    dve.wait_ge(v_rounded, TOK * pair + t + 1)
                    nc.vector.scalar_tensor_tensor(out=v_lo[:, t, :], in0=bank(s, t * GW, GW), scalar=rstd_mem[:, t:t + 1],
                                                   in1=v_hi[:, t, :].bitcast(F32), op0=ALU.mult,
                                                   op1=ALU.subtract).then_inc(v_split, 1)
                lo_units(u, 4, 9)
                lo_plain(yT_lo, yT_hi, pair * HALF, s, 4, HI[f"pv{pair}"])
                lo_units(u, 9, KD)
            u = UNIT0["xo1"]
            resid("xo0", 0, 1.0, "g_ffn2", u, by_dve=True)
            lo_units(u, LATE, KD)
            u = UNIT0["ffn2_in0"]
            resid("xo1", 1, 1.0, "g_ffn2", u)
            dve.wait_ge(squared, SQUARED["xo1"] + 2)
            norm("xo", halves, D, rstd[:, :])
            lo_units(u, 8, KD)
            ffn_in(2)
            ffn_out(2)
            u = UNIT0["ffn2_out1"]
            lo_units(u, 0, 4)
            add_resid("ffn2_out0", 0, 0.5)
            lo_units(u, 4, 8)
            dve.wait_ge(gfin_loaded, 16)
            dve.wait_ge(squared, SQUARED["ffn2_out0"] + TOK)
            for t in range(TOK):
                nc.vector.tensor_tensor(h[:, t, 0:GW], h[:, t, 0:GW], g_fin[:, 0:GW], ALU.mult).then_inc(gained, 1)
            lo_units(u, 8, KF)
            for t in range(TOK):
                for b in range(2):
                    n = 2 * t + b
                    hs = h[:, t, GW + b * BLK:GW + (b + 1) * BLK]
                    dve.wait_ge(last_block, n + 1)
                    nc.vector.scalar_tensor_tensor(out=hs, in0=bank(SET["ffn2_out1"], n * BLK, BLK), scalar=0.5, in1=hs,
                                                   op0=ALU.mult, op1=ALU.add).then_inc(staged, 1)
                    dve.wait_ge(staged, STAGED["ffn2_out1"] + n + 1)
                    nc.vector.tensor_tensor(stage[:, t, b * BLK:(b + 1) * BLK], hs, g_fin[:, GW + b * BLK:GW + (b + 1) * BLK],
                                            ALU.mult).then_inc(gained, 1)
                    dve.wait_ge(squared, SQUARED["ffn2_out1"] + n + 1)
                    if b == 0:
                        part = ms_part[:, t:t + 1]
                        chain(nc.vector.tensor_tensor(part, ssq[:, 0, t:t + 1], ssq_end[:, t, 0:1], ALU.add))
                        chain(nc.vector.tensor_scalar(part, part, 1.0 / D, EPS, ALU.mult, ALU.add))
                ms, rt, inv, r = (small[:, i, 0:1] for i in range(4))
                nc.vector.scalar_tensor_tensor(out=ms, in0=ssq_end[:, t, 1:2], scalar=1.0 / D, in1=part,
                                               op0=ALU.mult, op1=ALU.add).then_inc(ms_ready, 1)
                dve.wait_ge(root_ready, NORM[f"final{t}"] + 1)
                chain(nc.vector.reciprocal(inv, rt))
                chain(nc.vector.scalar_tensor_tensor(out=r, in0=inv, scalar=ms, in1=inv, op0=ALU.mult, op1=ALU.mult))
                chain(nc.vector.tensor_scalar(r, r, -0.5, 1.5, ALU.mult, ALU.add))
                nc.vector.tensor_tensor(rstd[:, t:t + 1], inv, r, ALU.mult).then_inc(rstd_ready, 1)
                dve.wait_ge(rstd_ready, NORM[f"final{t}"] + 1)
                nc.vector.tensor_scalar(h[:, t, 0:GW], h[:, t, 0:GW], rstd[:, t:t + 1], None,
                                        ALU.mult).then_inc(out_ready[0], 1)

        @block.tensor
        def _(pe):
            def mul_units(unit0, n, k0, k1, T_hi, T_lo, s, only=None):
                for k in range(k0, k1):
                    pe.wait_ge(lo_ready, unit0 + (k + 1))
                    for t in range(TOK) if only is None else only[:1]:
                        for xs, ws_ in ((T_hi, w_hi), (T_hi, w_lo), (T_lo, w_hi)):
                            for b in range(2) if only is None else only[1:]:
                                ins = nc.tensor.matmul(bank(s, t * GW + b * BLK, BLK), xs[:, k, t * P:(t + 1) * P],
                                                       ws_[:, k % RING, b * BLK:(b + 1) * BLK],
                                                       start=(k == 0 and xs is T_hi and ws_ is w_hi),
                                                       stop=(k == n - 1 and xs is T_lo))
                    if only is None:
                        ins.then_inc(unit_used, 1)
                    elif k == n - 1:
                        ins.then_inc(last_block, 1)

            def turn(src, s, k1, k0=0):
                for k in range(k0, k1):
                    for t in range(TOK):
                        ins = nc.tensor.transpose(bank(s, k * SEQ + t * P, P), src(k, t), ident[:, :])
                    if k % 2 == 1:
                        ins.then_inc(turned, 1)

            def from_stage(k, t):
                return stage[:, t, k * P:(k + 1) * P]

            def from_half(a, c):
                return lambda k, t: a[:, t, c * GW + k * P:c * GW + (k + 1) * P]

            def group(name, T_hi, T_lo, k0, k1, only=None):
                mul_units(UNIT0[name], UNITS[name], k0, k1, T_hi, T_lo, SET[name], only)

            def mul_split(out, lhs, rhs, first, last):
                for n, (a, b) in enumerate(((0, 0), (0, 1), (1, 0))):
                    ins = nc.tensor.matmul(out, lhs[a], rhs[b], start=first and n == 0, stop=last and n == 2)
                return ins

            def ffn_in(f):
                u0 = UNIT0[f"ffn{f}_in0"]
                with pe.Fori(0, FG // 2) as i:
                    for j in range(2):
                        unit0 = i * (2 * KD) + (u0 + (1 + j) * KD)
                        s = (1 + j) % 2
                        if j == 0:
                            pe.wait_ge(taken, i * 4 + TAKEN[f"ffn{f}_in0"])
                        else:
                            pe.wait_ge(taken, i * 4 + (TAKEN[f"ffn{f}_in0"] + 2))
                        mul_units(unit0, KD, 0, KD, xT_hi, xT_lo, s)

            def ffn_out(f):
                last = f"ffn{f}_in{FG - 1}"
                a, b = f"ffn{f}_out0", f"ffn{f}_out1"
                pe.wait_ge(taken, TAKEN[last])
                group(a, hidT_hi, hidT_lo, 0, KF - 4)
                pe.wait_ge(taken, TAKEN[last] + 2)
                group(a, hidT_hi, hidT_lo, KF - 4, KF)
                if f == 1:
                    group(b, hidT_hi, hidT_lo, 0, KF)
                else:
                    group(b, hidT_hi, hidT_lo, 0, KF - RING)
                    for n in range(4):
                        group(b, hidT_hi, hidT_lo, KF - RING, KF, only=(n // 2, n % 2))

            def resid(name, c, first, T_hi, T_lo, before):
                pe.wait_ge(taken, before)
                group(first, T_hi, T_lo, 0, 4)
                pe.wait_ge(staged, STAGED[name] + TOK)
                turn(from_half(h, c), SET[name], HALF)
                group(first, T_hi, T_lo, 4, 8)

            pe.wait_ge(ident_ready, 1)
            pe.wait_ge(gain_loaded, 16)
            nc.tensor.transpose(bank(0, 0, KD), rows[0:KD, :], ident[0:KD, 0:KD]).then_inc(rows_turned, 1)
            for q in range(2):
                pe.wait_ge(x_loaded[q], 16)
                turn(from_half(h, 0), 1, 4 * q + 4, 4 * q)
                pe.wait_ge(cols_ready, 1)
                pe.wait_ge(taken, TAKEN["x0"] + q + 1)
                group("ffn1_in0", xT_hi, xT_lo, 2 * q, 2 * q + 2)
            for q in range(2):
                pe.wait_ge(x_loaded[2 + q], 16)
                pe.wait_ge(taken, TAKEN["x0"] + 3 + q)
                turn(from_half(h, 1), 1, 4 * q + 4, 4 * q)
                group("ffn1_in0", xT_hi, xT_lo, 4 + 2 * q, 6 + 2 * q)
            for q in range(2):
                pe.wait_ge(taken, TAKEN["x1"] + 2 * q + 2)
                group("ffn1_in0", xT_hi, xT_lo, 8 + 2 * q, 10 + 2 * q)
            pe.wait_ge(rows_loaded, 16 * (len(vectors) - 1))
            nc.tensor.transpose(bank(1, 0, NROWS), rows[0:NROWS, :], ident[0:NROWS, 0:NROWS]).then_inc(rows_turned, 1)
            group("ffn1_in0", xT_hi, xT_lo, 12, KD)
            pe.wait_ge(cols_ready, 2)
            ffn_in(1)
            ffn_out(1)
            resid("ffn1_out1", 1, "C", xT_hi, xT_lo, TAKEN["ffn1_out0"] + 4)
            pe.wait_ge(taken, TAKEN["ffn1_out1"] + 4)
            group("C", xT_hi, xT_lo, 8, 9)
            pe.wait_ge(ws_masked, 1)
            for hd in range(HEADS):
                ins = nc.tensor.transpose(bank(SET["ffn1_out1"], hd * P, P), ws[:, hd, :], ident[:, :])
                if hd % 4 == 3:
                    ins.then_inc(turned, 1)
            group("C", xT_hi, xT_lo, 9, KD)
            pe.wait_ge(taken, TAKEN["ws"] + 2)
            group("H", xT_hi, xT_lo, 0, KD)
            pe.wait_ge(c_taken, TOK)
            group("B", xT_hi, xT_lo, 0, KD)
            pe.wait_ge(z_taken, HALF)
            group("V", xT_hi, xT_lo, 0, KD)
            pe.wait_ge(yc_product, 1)
            group("U", xT_hi, xT_lo, 0, 10)
            pe.wait_ge(vn_ready, TOK)
            for hd in range(HEADS):
                ins = nc.tensor.matmul(bank(SET["V"], hd * SEQ, SEQ), wsT[:, hd, :], v_buf[:, :, hd * P:(hd + 1) * P],
                                       start=True, stop=True)
                if hd % 2 == 1:
                    ins.then_inc(gated, 1)
            group("U", xT_hi, xT_lo, 10, KD)
            pe.wait_ge(sg_ready, HEADS)
            pe.wait_ge(yc_ready, 1)
            group("mix_out0", yT_hi, yT_lo, 0, 4)
            pe.wait_ge(staged, STAGED["U"] + TOK)
            turn(from_stage, SET["U"], HALF)
            group("mix_out0", yT_hi, yT_lo, 4, 8)
            pe.wait_ge(taken, TAKEN["U"] + 4)
            group("mix_out0", yT_hi, yT_lo, 8, KD)
            resid("mix_out0", 0, "mix_out1", yT_hi, yT_lo, TAKEN["U"] + 4)
            group("mix_out1", yT_hi, yT_lo, 8, 9)
            pe.wait_ge(taken, TAKEN["mix_out0"] + 4)
            pe.wait_ge(mem_loaded, 16)
            turn(from_half(mem_nat, 0), SET["mix_out0"], HALF)
            group("mix_out1", yT_hi, yT_lo, 9, KD)
            resid("mix_out1", 1, "q0", xT_hi, xT_lo, TAKEN["memA"] + 4)
            pe.wait_ge(taken, TAKEN["mix_out1"] + 4)
            group("q0", xT_hi, xT_lo, 8, 9)
            turn(from_half(mem_nat, 1), SET["mix_out1"], HALF)
            group("q0", xT_hi, xT_lo, 9, KD)

            def turned_group(name, T_hi, T_lo, before, running, k1):
                pe.wait_ge(taken, before)
                group(running, T_hi, T_lo, 0, 4)
                pe.wait_ge(staged, STAGED[name] + TOK)
                turn(from_stage, SET[name], HALF)
                group(running, T_hi, T_lo, 4, k1)

            def scores(pair):
                pe.wait_ge(taken, TAKEN[f"k{pair}"] + 4)
                for j in range(4):
                    for d in range(DT):
                        k = pair * HALF + (j // 2) * DT + d
                        tok = slice((j % 2) * P, (j % 2 + 1) * P)
                        ins = mul_split(bank(SET[f"k{pair}"], j * SEQ, SEQ), (qT_hi[:, k, tok], qT_lo[:, k, tok]),
                                        (kT_hi[:, k, :], kT_lo[:, k, :]), d == 0, d == DT - 1)
                ins.then_inc(scored, 1)

            def turn_probs(pair):
                pe.wait_ge(probs_ready, pair + 1)
                for hd in range(2):
                    for m in range(2):
                        for t in range(TOK):
                            at = (hd * 2 + t) * SEQ + m * P
                            ins = nc.tensor.transpose(bank(SET[f"k{pair}"], GW + (hd * 2 + m) * SEQ + t * P, P),
                                                      scratch[:, at:at + P], ident[:, :])
                    ins.then_inc(turned, 1)

            def attend(pair):
                pe.wait_ge(v_split, TOK * (pair + 1))
                pe.wait_ge(taken, TAKEN[f"p{pair}"] + 2)
                for d in range(2 * DT):
                    for m in range(2):
                        dc = slice(d * P, (d + 1) * P)
                        tile = 4 * pair + 2 * (d // DT) + m
                        ins = mul_split(bank(SET[f"v{pair}"], d * SEQ, SEQ), (v_hi[:, m, dc], v_lo[:, m, dc]),
                                        (pT_hi[:, tile, :], pT_lo[:, tile, :]), m == 0, m == 1)
                    if d % 2 == 1:
                        ins.then_inc(pv_done, 1)

            pe.wait_ge(taken, TAKEN["memB"] + 4)
            group("q1", xT_hi, xT_lo, 0, KD)
            pe.wait_ge(taken, TAKEN["q0"] + 4)
            group("k0", memT_hi, memT_lo, 0, KD)
            turned_group("k0", memT_hi, memT_lo, TAKEN["q1"] + 4, "k1", 7)
            for pair, running in enumerate(("k1", "v0")):
                if pair == 1:
                    turned_group("k1", memT_hi, memT_lo, TAKEN["p0"] + 2, "v0", 7)
                scores(pair)
                group(running, memT_hi, memT_lo, 7, 11)
                turn_probs(pair)
                group(running, memT_hi, memT_lo, 11, KD)
            pe.wait_ge(taken, TAKEN["p1"] + 2)
            group("v1", memT_hi, memT_lo, 0, 5)
            attend(0)
            group("v1", memT_hi, memT_lo, 5, KD)
            pe.wait_ge(taken, TAKEN["pv0"] + 4)
            group("xo0", yT_hi, yT_lo, 0, 5)
            attend(1)
            group("xo0", yT_hi, yT_lo, 5, 8)
            pe.wait_ge(taken, TAKEN["pv1"] + 4)
            group("xo0", yT_hi, yT_lo, 8, KD)
            group("xo1", yT_hi, yT_lo, 0, KD)
            resid("xo1", 1, "ffn2_in0", xT_hi, xT_lo, TAKEN["xo0"] + 4)
            pe.wait_ge(taken, TAKEN["xo1"] + 4)
            group("ffn2_in0", xT_hi, xT_lo, 8, KD)
            ffn_in(2)
            ffn_out(2)


_INS = ["x", "mem", "g_ffn1", "w_ffn1_in", "w_ffn1_out", "g_mix", "w_mix_in", "conv_w", "conv_b", "g_gm_v", "w_spatial",
        "b_spatial", "w_mix_out", "g_xattn", "g_mem", "w_xq", "w_xk", "w_xv", "w_xo", "g_ffn2", "w_ffn2_in",
        "w_ffn2_out", "g_final"]


def kernel(**inputs):
    import numpy as np
    import concourse.bacc as bacc
    from concourse.bass_utils import run_bass_kernel_spmd

    nc = bacc.Bacc("TRN2", target_bir_lowering=False, num_devices=1)
    arrays, args = {}, []
    for name in _INS:
        a = np.ascontiguousarray(inputs[name])
        arrays[f"in_{name}"] = a
        args.append(nc.dram_tensor(f"in_{name}", a.shape, mybir.dt.from_np(a.dtype), kind="ExternalInput").ap())
    shape = arrays["in_x"].shape
    args.append(nc.dram_tensor("out_0", shape, F32, kind="ExternalOutput").ap())
    build(nc, *args)
    r = run_bass_kernel_spmd(nc, [arrays], core_ids=[0])
    return r.results[0]["out_0"]
```
